# Optimizing a Trainium2 kernel written in Bass

```python
import jax, jax.numpy as jnp
from jax import lax
import numpy as np

D_MODEL = 1024
BATCH = 1
SEQ = 256
DEPTH = 2

D_MIX = D_MODEL
MLA_HEADS = 8
NOPE_DIM = 64
ROPE_DIM = 32
V_DIM = 64
QK_DIM = NOPE_DIM + ROPE_DIM
Q_RANK = 256
KV_RANK = 128
MLA_WIDTH = MLA_HEADS * V_DIM
LRU_WIDTH = D_MIX - MLA_WIDTH
LRU_BLOCKS = 8
LRU_BLOCK = LRU_WIDTH // LRU_BLOCKS
CONV_WIDTH = 4
LRU_C = 8.0
IN_SPLITS = (Q_RANK, Q_RANK + KV_RANK, Q_RANK + KV_RANK + ROPE_DIM,
             Q_RANK + KV_RANK + ROPE_DIM + LRU_WIDTH)
IN_COLS = Q_RANK + KV_RANK + ROPE_DIM + 2 * LRU_WIDTH
D_FF = 2816
N_EXPERTS = 8
TOP_K = 2
D_FF_EXPERT = 3584
N_DENSE = (DEPTH + 1) // 2
N_MOE = DEPTH // 2
ROPE_THETA = 10000.0
Q_BLOCK = 128
EPS = 1e-6

kernel_name = "hymba_mla_rglru_moe_adaln_trunk"

def _rms(x, gain):
    xf = x.astype(jnp.float32)
    y = xf * lax.rsqrt(jnp.mean(xf * xf, axis=-1, keepdims=True) + EPS)
    return (y * gain.astype(jnp.float32)).astype(x.dtype)

def _rope(x, cos, sin):
    x1, x2 = jnp.split(x, 2, axis=-1)
    return jnp.concatenate([x1 * cos - x2 * sin, x1 * sin + x2 * cos], axis=-1)

def _modulate(c_act, w, b):
    m = (c_act @ w + b)[:, None, :]
    shift, scale, gate = jnp.split(m, 3, axis=-1)
    return shift, scale, gate

def _causal_attention(q, k, v, positions):
    B, S, H, _ = q.shape
    nb = S // Q_BLOCK
    qb = q.reshape(B, nb, Q_BLOCK, H, QK_DIM).transpose(1, 0, 2, 3, 4)
    pb = positions.reshape(B, nb, Q_BLOCK).transpose(1, 0, 2)
    scale = QK_DIM ** -0.5
    neg = jnp.finfo(jnp.float32).min

    def one_block(args):
        q_blk, p_blk = args
        s = jnp.einsum('bqhd,bkhd->bhqk', q_blk, k,
                       preferred_element_type=jnp.float32) * scale
        mask = positions[:, None, None, :] <= p_blk[:, None, :, None]
        p = jax.nn.softmax(jnp.where(mask, s, neg), axis=-1).astype(v.dtype)
        return jnp.einsum('bhqk,bkhd->bqhd', p, v)

    o = lax.map(one_block, (qb, pb))
    return o.transpose(1, 0, 2, 3, 4).reshape(B, S, H * V_DIM)

def _causal_conv(x, w, b):
    y = lax.conv_general_dilated(
        x, w[:, None, :].astype(x.dtype), window_strides=(1,),
        padding=[(CONV_WIDTH - 1, 0)], dimension_numbers=('NWC', 'WIO', 'NWC'),
        feature_group_count=x.shape[-1])
    return y + b

def _rglru(x, w_a, b_a, w_x, b_x, lam):
    B, S, _ = x.shape
    xb = x.reshape(B, S, LRU_BLOCKS, LRU_BLOCK)
    r = jax.nn.sigmoid((jnp.einsum('bsgi,gij->bsgj', xb, w_a).reshape(B, S, LRU_WIDTH) + b_a).astype(jnp.float32))
    i = jax.nn.sigmoid((jnp.einsum('bsgi,gij->bsgj', xb, w_x).reshape(B, S, LRU_WIDTH) + b_x).astype(jnp.float32))
    log_a = LRU_C * r * jax.nn.log_sigmoid(lam.astype(jnp.float32))
    a = jnp.exp(log_a)
    u = jnp.sqrt(-jnp.expm1(2.0 * log_a)) * (i * x.astype(jnp.float32))

    def combine(left, right):
        a1, b1 = left
        a2, b2 = right
        return a1 * a2, a2 * b1 + b2

    _, h = lax.associative_scan(combine, (a, u), axis=1)
    return h.astype(x.dtype)

def _hybrid_mixer(h, positions, cos, sin, w_in, latent_gain, w_q_up, w_kv_up, q_gain, k_gain,
                  conv_w, conv_b, w_a, b_a, w_x, b_x, lam, out_gain, w_out):
    B, S, _ = h.shape
    z = h @ w_in
    c_q, c_kv, k_r, x_rec, g_rec = jnp.split(z, IN_SPLITS, axis=-1)
    c_q = _rms(c_q, latent_gain[:Q_RANK])
    c_kv = _rms(c_kv, latent_gain[Q_RANK:])
    q = (c_q @ w_q_up).reshape(B, S, MLA_HEADS, QK_DIM)
    kv = (c_kv @ w_kv_up).reshape(B, S, MLA_HEADS, NOPE_DIM + V_DIM)
    k_nope, v = kv[..., :NOPE_DIM], kv[..., NOPE_DIM:]
    q_nope = _rms(q[..., :NOPE_DIM], q_gain[:NOPE_DIM])
    q_rope = _rope(_rms(q[..., NOPE_DIM:], q_gain[NOPE_DIM:]), cos[:, :, None, :], sin[:, :, None, :])
    k_nope = _rms(k_nope, k_gain[:NOPE_DIM])
    k_rope = _rope(_rms(k_r, k_gain[NOPE_DIM:]), cos, sin)
    qf = jnp.concatenate([q_nope, q_rope], axis=-1)
    kf = jnp.concatenate([k_nope, jnp.broadcast_to(k_rope[:, :, None, :], (B, S, MLA_HEADS, ROPE_DIM))], axis=-1)
    attn = _causal_attention(qf, kf, v, positions)
    xr = _causal_conv(x_rec, conv_w, conv_b)
    rec = _rglru(xr, w_a, b_a, w_x, b_x, lam) * jax.nn.gelu(g_rec)
    y = jnp.concatenate([_rms(attn, out_gain[:MLA_WIDTH]), _rms(rec, out_gain[MLA_WIDTH:])], axis=-1)
    return y @ w_out

def _swiglu(h, wg, wu, wd):
    return (jax.nn.silu(h @ wg) * (h @ wu)) @ wd

def _moe(h, w_router, wg, wu, wd):
    B, S, D = h.shape
    t = h.reshape(B * S, D)
    logits = (t @ w_router).astype(jnp.float32)
    top_val, top_idx = lax.top_k(logits, TOP_K)
    top_w = jax.nn.softmax(top_val, axis=-1)
    combine = jnp.sum(jax.nn.one_hot(top_idx, N_EXPERTS, dtype=jnp.float32) * top_w[..., None], axis=1)
    combine = combine.astype(t.dtype)
    out = jnp.zeros_like(t)
    for e in range(N_EXPERTS):
        out = out + combine[:, e:e + 1] * _swiglu(t, wg[e], wu[e], wd[e])
    return out.reshape(B, S, D)

def setup_inputs(seed: int = 0) -> dict:
    key = jax.random.key(seed)
    ks = jax.random.split(key, 32)
    f32 = jnp.float32

    def nrm(k, shape, fan_in):
        return jax.random.normal(k, shape, f32) * (fan_in ** -0.5)

    def gain(k, shape):
        return 1.0 + 0.02 * jax.random.normal(k, shape, f32)

    x = jax.random.normal(ks[0], (BATCH, SEQ, D_MODEL), f32)
    c = jax.random.normal(ks[1], (BATCH, D_MODEL), f32)
    offset = jax.random.randint(ks[2], (BATCH, 1), 0, 1024, dtype=jnp.int32)
    positions = offset + jnp.arange(SEQ, dtype=jnp.int32)[None, :]

    w_ada = jax.random.normal(ks[3], (DEPTH, 2, D_MODEL, 3 * D_MODEL), f32) * (0.1 * D_MODEL ** -0.5)
    gate_offset = jnp.concatenate([jnp.zeros((2 * D_MODEL,), f32), jnp.ones((D_MODEL,), f32)])
    b_ada = 0.02 * jax.random.normal(ks[4], (DEPTH, 2, 3 * D_MODEL), f32) + gate_offset
    norm_gain = gain(ks[5], (DEPTH, 2, D_MODEL))

    w_in = nrm(ks[6], (DEPTH, D_MODEL, IN_COLS), D_MODEL)
    latent_gain = gain(ks[7], (DEPTH, Q_RANK + KV_RANK))
    w_q_up = nrm(ks[8], (DEPTH, Q_RANK, MLA_HEADS * QK_DIM), Q_RANK)
    w_kv_up = nrm(ks[9], (DEPTH, KV_RANK, MLA_HEADS * (NOPE_DIM + V_DIM)), KV_RANK)
    q_gain = gain(ks[10], (DEPTH, QK_DIM))
    k_gain = gain(ks[11], (DEPTH, QK_DIM))

    conv_w = nrm(ks[12], (DEPTH, CONV_WIDTH, LRU_WIDTH), CONV_WIDTH)
    conv_b = 0.01 * jax.random.normal(ks[13], (DEPTH, LRU_WIDTH), f32)
    w_a = nrm(ks[14], (DEPTH, LRU_BLOCKS, LRU_BLOCK, LRU_BLOCK), LRU_BLOCK)
    b_a = 0.01 * jax.random.normal(ks[15], (DEPTH, LRU_WIDTH), f32)
    w_x = nrm(ks[16], (DEPTH, LRU_BLOCKS, LRU_BLOCK, LRU_BLOCK), LRU_BLOCK)
    b_x = 0.01 * jax.random.normal(ks[17], (DEPTH, LRU_WIDTH), f32)
    a8 = jax.random.uniform(ks[18], (DEPTH, LRU_WIDTH), f32, minval=0.9, maxval=0.999)
    a0 = a8 ** (1.0 / LRU_C)
    lru_lambda = jnp.log(a0) - jnp.log1p(-a0)

    out_gain = gain(ks[19], (DEPTH, D_MIX))
    w_out = nrm(ks[20], (DEPTH, D_MIX, D_MODEL), D_MIX)

    ffn_w_gate = nrm(ks[21], (N_DENSE, D_MODEL, D_FF), D_MODEL)
    ffn_w_up = nrm(ks[22], (N_DENSE, D_MODEL, D_FF), D_MODEL)
    ffn_w_down = nrm(ks[23], (N_DENSE, D_FF, D_MODEL), D_FF)

    router_w = nrm(ks[24], (N_MOE, D_MODEL, N_EXPERTS), D_MODEL)
    moe_w_gate = nrm(ks[25], (N_MOE, N_EXPERTS, D_MODEL, D_FF_EXPERT), D_MODEL)
    moe_w_up = nrm(ks[26], (N_MOE, N_EXPERTS, D_MODEL, D_FF_EXPERT), D_MODEL)
    moe_w_down = nrm(ks[27], (N_MOE, N_EXPERTS, D_FF_EXPERT, D_MODEL), D_FF_EXPERT)

    return {"x": x, "c": c, "positions": positions, "w_ada": w_ada, "b_ada": b_ada,
            "norm_gain": norm_gain, "w_in": w_in, "latent_gain": latent_gain, "w_q_up": w_q_up,
            "w_kv_up": w_kv_up, "q_gain": q_gain, "k_gain": k_gain, "conv_w": conv_w, "conv_b": conv_b,
            "w_a": w_a, "b_a": b_a, "w_x": w_x, "b_x": b_x, "lru_lambda": lru_lambda,
            "out_gain": out_gain, "w_out": w_out, "ffn_w_gate": ffn_w_gate, "ffn_w_up": ffn_w_up,
            "ffn_w_down": ffn_w_down, "router_w": router_w, "moe_w_gate": moe_w_gate,
            "moe_w_up": moe_w_up, "moe_w_down": moe_w_down}

def reference(x, c, positions, w_ada, b_ada, norm_gain, w_in, latent_gain, w_q_up, w_kv_up, q_gain,
              k_gain, conv_w, conv_b, w_a, b_a, w_x, b_x, lru_lambda, out_gain, w_out, ffn_w_gate,
              ffn_w_up, ffn_w_down, router_w, moe_w_gate, moe_w_up, moe_w_down):
    c_act = jax.nn.silu(c)
    inv_freq = ROPE_THETA ** (-jnp.arange(0, ROPE_DIM, 2, dtype=jnp.float32) / ROPE_DIM)
    ang = positions.astype(jnp.float32)[..., None] * inv_freq
    cos = jnp.cos(ang).astype(x.dtype)
    sin = jnp.sin(ang).astype(x.dtype)
    for l in range(DEPTH):
        shift, scale, gate = _modulate(c_act, w_ada[l, 0], b_ada[l, 0])
        h = _rms(x, norm_gain[l, 0]) * (1.0 + scale) + shift
        x = x + gate * _hybrid_mixer(h, positions, cos, sin, w_in[l], latent_gain[l], w_q_up[l],
                                     w_kv_up[l], q_gain[l], k_gain[l], conv_w[l], conv_b[l], w_a[l],
                                     b_a[l], w_x[l], b_x[l], lru_lambda[l], out_gain[l], w_out[l])
        shift, scale, gate = _modulate(c_act, w_ada[l, 1], b_ada[l, 1])
        h = _rms(x, norm_gain[l, 1]) * (1.0 + scale) + shift
        if l % 2 == 0:
            j = l // 2
            f = _swiglu(h, ffn_w_gate[j], ffn_w_up[j], ffn_w_down[j])
        else:
            j = l // 2
            f = _moe(h, router_w[j], moe_w_gate[j], moe_w_up[j], moe_w_down[j])
        x = x + gate * f
    return x


_drawn_inputs = setup_inputs


def setup_inputs(seed=0):
    import zlib

    import numpy as np

    out = dict(_drawn_inputs(seed))
    spreads = {}
    factors = {'k_gain': 2.852, 'b_a': 19.102, 'b_x': 6.325}
    for name, (base, spread) in spreads.items():
        noise = np.random.default_rng([zlib.crc32(name.encode()), seed]).standard_normal(out[name].shape)
        drawn = base * np.exp(spread * noise) if base else spread * noise
        out[name] = __import__('jax').numpy.asarray(drawn.astype(out[name].dtype))
    for name, factor in factors.items():
        out[name] = (out[name] * factor).astype(out[name].dtype)
    return out
```

```python
from contextlib import ExitStack

import numpy as np

import concourse.bass as bass
from concourse import mybir
from concourse.alu_op_type import AluOpType as ALU

F32 = mybir.dt.float32
I32 = mybir.dt.int32
U32 = mybir.dt.uint32
ACT = mybir.ActivationFunctionType
AX = mybir.AxisListType.X

P = 128
EPS = 1e-6
NEG = -1e30
GELU_A = 0.044715
GELU_B = float(np.sqrt(2.0 / np.pi))
SLOTS = 7
FT = 2
BLK = 64
TWO_PI = 2.0 * np.pi


def cody_waite():
    c1 = 6.28125
    c2 = float(np.round((TWO_PI - c1) * 2.0 ** 21) / 2.0 ** 21)
    return c1, c2, float(np.float32(TWO_PI - c1 - c2))


def trunk(nc, x_in, c_in, pos_in, w_ada, b_ada, norm_gain, w_in, latent_gain, w_q_up, w_kv_up, q_gain, k_gain,
          conv_w, conv_b, w_a, b_a, w_x, b_x, lru_lambda, out_gain, w_out, ffn_gate, ffn_up, ffn_down,
          router_w, moe_gate, moe_up, moe_down, out):
    _, SEQ, D = x_in.shape
    DEPTH = w_ada.shape[0]
    IN_COLS = w_in.shape[2]
    Q_RANK = w_q_up.shape[1]
    KV_RANK = w_kv_up.shape[1]
    LRU = conv_w.shape[2]
    TAPS = conv_w.shape[1]
    QK = q_gain.shape[1]
    NOPE = 64
    ROPE = QK - NOPE
    HALF = ROPE // 2
    H = w_q_up.shape[2] // QK
    V = w_kv_up.shape[2] // H - NOPE
    D_FF = ffn_gate.shape[2]
    NE = router_w.shape[2]
    D_FFE = moe_gate.shape[3]
    LAT = Q_RANK + KV_RANK + ROPE
    NT = SEQ // P
    KD = D // P
    LT = LRU // P
    CHUNKS = D_FF // (FT * P)
    ECHUNKS = D_FFE // (FT * P)
    EH = ECHUNKS // SLOTS
    NBLK = SEQ // BLK
    FW = FT * P
    SCALE = float(QK) ** -0.5
    assert NT == 2 and KD == 8 and LT == 4 and H == 8 and V == 64 and D_FF % FW == 0 and ECHUNKS % SLOTS == 0
    assert EH == 2 and DEPTH == 2 and Q_RANK == 256 and KV_RANK == 128
    inv_freq = [float(np.float32(1e4) ** np.float32(-2 * i / ROPE)) for i in range(HALF)]

    with ExitStack() as ctx:
        def sb(name, cols, dt=F32):
            return ctx.enter_context(nc.sbuf_tensor(name, [P, cols], dt))

        sems = {}

        def sem(name):
            if name not in sems:
                sems[name] = ctx.enter_context(nc.semaphore(name))
            return sems[name]

        ps = ctx.enter_context(nc.psum_tensor("ps", [P, 8, 512], F32))
        SW_ = 3 * FT * KD * P
        ring = ctx.enter_context(nc.sbuf_tensor("ring", [P, SLOTS, SW_], F32))
        WORK0 = 4
        work = ring[:, WORK0:SLOTS, :].rearrange("p s n -> p (s n)")
        x = sb("x", NT * D)[:, :].rearrange("p (t d) -> p t d", t=NT)
        hT = sb("hT", KD * SEQ)[:, :].rearrange("p (k n) -> p k n", k=KD)
        F = sb("F", 4992)
        ident = sb("ident", P)
        ones = sb("ones", P)
        zero = sb("zero", 2)
        iota = sb("iota", SEQ)
        colA = sb("colA", 126)
        colB = sb("colB", 96)
        adav = sb("adav", 4 * 24)[:, :].rearrange("p (a n) -> p a n", a=4)
        adaA = sb("adaA", 4 * KD)[:, :].rearrange("p (a n) -> p a n", a=4)
        cact = sb("cact", KD)
        hb = sb("hb", 16)
        m2ls = sb("m2ls", 2 * LT)
        st = sb("st", 48)
        rs = sb("rs", 48)
        mx = sb("mx", 2 * H)
        den = sb("den", 2 * H)
        mark = sb("mark", 16)
        posm = sb("posm", NT * NE)[:, :].rearrange("p (t e) -> p t e", t=NT)
        wts = sb("wts", NT * NE)[:, :].rearrange("p (t e) -> p t e", t=NT)
        meta = sb("meta", 2 * NE, I32)

        def part(buf, at, *dims):
            n = int(np.prod(dims))
            v = buf[:, at:at + n]
            if len(dims) == 1:
                return v
            names = "abcd"[:len(dims)]
            return v.rearrange(f"p ({' '.join(names)}) -> p {' '.join(names)}",
                               **{k: d for k, d in zip(names[1:], dims[1:])})

        xn = part(F, 0, NT, D)
        xp = part(F, 0, LT, SEQ + TAPS - 1)
        gr = part(F, 1036, LT, SEQ)
        lq = part(F, 2060, LT, SEQ)
        cT = part(F, 3084, 3, SEQ)
        mask = part(F, 3852, SEQ)
        gains = part(F, 4108, 4, QK)
        cs = part(F, 4492, NT, 2, HALF)
        rw = part(F, 4556, KD, NE)
        tri = part(F, 4620, P)
        wq = part(work, 0, 2, H * QK)
        wkv = part(work, 1536, H * (NOPE + V))
        wbd = part(work, 2560, 2, LT, P)
        kT = part(work, 3584, H, SEQ)
        mT = part(work, 3584, KD, SEQ)
        qn = part(work, 5632, NT, H, QK)
        kn = part(work, 7168, NT, H, QK)
        PT = part(work, 5632, NT + 1, H, P)
        v_sb = part(work, 8704, NT, H * V)
        s1 = part(work, 9728, H, SEQ)
        s0 = part(work, 11776, H, P)
        osb = part(work, 9728, NT, H, V)
        rbc = part(work, 9728 + NT * H * V, SEQ)
        sq = part(work, 12800, 832)
        cn = part(work, 12800, NT, LAT)
        lx = part(work, 13632, LT, SEQ)
        la = part(work, 14656, LT, SEQ)
        li = part(work, 15680, LT, SEQ)
        lr = part(work, 16704, LT, SEQ)
        rope_tmp = part(work, 17728, 4, H, HALF)
        qT = hT
        ygT = hT
        rowsA = part(work, 0, P)
        rowsB = part(work, P, P)
        f_tg = part(F, 0, FT, SEQ)
        f_hid = part(F, FT * SEQ, 2, FT, SEQ)
        hnat = part(F, 0, NT, D)
        e_tg = part(F, 2048, NBLK, FT * BLK)
        yT = part(F, 2048, KD, BLK)
        e_hid = part(F, 2560, 2, NBLK, FT * BLK)
        sel = part(F, 3584, NT, BLK)
        swT = part(F, 3712, NT * P)
        ynat = part(F, 3968, D)
        pos_i = sb("pos_i", NT, I32)
        pos_f = sb("pos_f", NT)
        ivf = part(work, 2 * P, HALF)
        ang = part(work, 3 * P, 2, NT, HALF)
        angk = part(work, 4 * P, 2, NT, HALF)

        C0, NG, OG, LG, CW, CB, BA, BX, LM = 0, 8, 40, 56, 62, 94, 102, 110, 118

        def ada_fill(a, i, slot, *waits):
            return ("ada", a, i, slot, waits)
        FB = CHUNKS
        fills = [ada_fill(0, i, i) for i in range(4)] + [
            ("win", 0, 0, 0, (("ada_step0", 2),)),
            ("win", 0, 1, 1, (("ada_step0", 3),)),
            ("small", 0, 0, None, (("wbd_zero", 1),)),
            ada_fill(1, 0, 2, ("ada_step0", 4)),
            ada_fill(1, 1, 3, ("ada_red", 1)),
            ada_fill(1, 2, 2, ("ada_step1", 2)),
            ada_fill(1, 3, 3, ("ada_step1", 3)),
            ("wout", 0, 0, 0, (("z_done", 1),)),
            ("wout", 0, 1, 1, ()),
            ("ffn", 0, 0, 2, (("ada_step1", 4),)),
            ("ffn", 0, 1, 4, (("wout_done", 1),)),
            ("ffn", 0, 2, 5, ()),
            ("ffn", 0, 3, 6, ()),
            ("ffn", 0, 4, 0, ()),
            ("ffn", 0, 5, 1, ()),
            ("ffn", 0, 6, 3, (("ada_red", 2),)),
            ("ffn", 0, 7, 2, (("f_used", 1),)),
            ("ffn", 0, 8, 4, (("f_used", 2),)),
            ("ffn", 0, 9, 5, (("f_used", 3),)),
            ("ffn", 0, 10, 6, (("f_used", 4),)),
            ada_fill(2, 0, 0, ("f_used", 5)),
            ada_fill(2, 1, 1, ("f_used", 6)),
            ada_fill(2, 2, 0, ("ada_step1", 6)),
            ada_fill(2, 3, 1, ("ada_step1", 7)),
            ("win", 1, 0, 0, (("ada_step1", 8),)),
            ("win", 1, 1, 3, (("f_used", 7),)),
            ("small", 1, 0, None, (("wbd_zero", 2), ("f_used", 11))),
            ada_fill(3, 0, 2, ("f_used", 8)),
            ada_fill(3, 1, 1, ("ada_red", 3)),
            ada_fill(3, 2, 2, ("ada_step1", 10)),
            ada_fill(3, 3, 1, ("ada_step1", 11)),
            ("wout", 1, 0, 0, (("z_done", 2),)),
            ("wout", 1, 1, 3, ()),
            ("moe", 0, 2, 2, (("ada_step1", 12),)),
            ("moe", 0, 0, 0, (("wout_done", 2),)),
            ("moe", 0, 3, 3, ()),
            ("moe", 0, 4, 4, ()),
            ("moe", 0, 5, 5, ()),
            ("moe", 0, 6, 6, ()),
            ("moe", 0, 1, 1, (("ada_red", 4),)),
        ]
        assert FB == 11
        n_dma = {"ada": 1, "win": 1, "wout": 1, "ffn": 3, "moe": 3, "small": 6}
        landed, total = {}, {}
        for kind, a, i, slot, _ in fills:
            total[slot] = total.get(slot, 0) + 16 * n_dma[kind]
            landed[kind, a, i] = (slot, total[slot])
        before_moe = {s: total[s] - 48 for s in range(SLOTS)}

        def slot_sem(slot):
            return sem("small_in" if slot is None else f"slot{slot}_in")

        def wait_fill(eng, kind, a, i):
            slot, value = landed[kind, a, i]
            eng.wait_ge(slot_sem(slot), value)
            return slot

        def slot_parts(slot):
            g = ring[:, slot, 0:KD * FW].rearrange("p (k n) -> p k n", k=KD)
            u = ring[:, slot, KD * FW:2 * KD * FW].rearrange("p (k n) -> p k n", k=KD)
            d = ring[:, slot, 2 * KD * FW:].rearrange("p (f n) -> p f n", f=FT)
            return g, u, d

        def bank2(b, n=2):
            return ps[:, b:b + n, :].rearrange("p b n -> p (b n)")

        block = ctx.enter_context(nc.Block())

        @block.sync
        def _(sp):
            sp.dma_start(x[:, :, :], x_in[0].rearrange("(t p) d -> p t d", p=P)).then_inc(sem("x_in"), 16)

            def chunk(slot, wg, wu, wd, f0):
                g, u, d = slot_parts(slot)
                sp.dma_start(g, wg[:, bass.ds(f0, FW)].rearrange("(k p) f -> p k f", p=P)).then_inc(slot_sem(slot), 16)
                sp.dma_start(u, wu[:, bass.ds(f0, FW)].rearrange("(k p) f -> p k f", p=P)).then_inc(slot_sem(slot), 16)
                sp.dma_start(d, wd[bass.ds(f0, FW), :].rearrange("(f p) n -> p f n", p=P)).then_inc(slot_sem(slot), 16)

            def expert_chunk(slot, e, f0):
                g, u, d = slot_parts(slot)
                wg = moe_gate[0, bass.ds(e, 1), :, f0:f0 + FW].rearrange("e (k p) f -> p (e k) f", p=P)
                wu = moe_up[0, bass.ds(e, 1), :, f0:f0 + FW].rearrange("e (k p) f -> p (e k) f", p=P)
                wd = moe_down[0, bass.ds(e, 1), f0:f0 + FW, :].rearrange("e (f p) n -> p (e f) n", p=P)
                sp.dma_start(g, wg).then_inc(slot_sem(slot), 16)
                sp.dma_start(u, wu).then_inc(slot_sem(slot), 16)
                sp.dma_start(d, wd).then_inc(slot_sem(slot), 16)

            for kind, a, i, slot, waits in fills:
                for name, value in waits:
                    sp.wait_ge(sem(name), value)
                if kind == "ada":
                    src = w_ada[a // 2, a % 2, i * 2 * P:(i + 1) * 2 * P, :].rearrange("(k p) n -> p k n", p=P)
                    dst = ring[:, slot, :].rearrange("p (k n) -> p k n", k=2)
                    sp.dma_start(dst, src).then_inc(slot_sem(slot), 16)
                elif kind == "win":
                    src = w_in[a, i * 4 * P:(i + 1) * 4 * P, :].rearrange("(k p) n -> p k n", p=P)
                    dst = ring[:, slot, 0:4 * IN_COLS].rearrange("p (k n) -> p k n", k=4)
                    sp.dma_start(dst, src).then_inc(slot_sem(slot), 16)
                elif kind == "wout":
                    src = w_out[a, i * 4 * P:(i + 1) * 4 * P, :].rearrange("(k p) n -> p k n", p=P)
                    dst = ring[:, slot, 0:4 * D].rearrange("p (k n) -> p k n", k=4)
                    sp.dma_start(dst, src).then_inc(slot_sem(slot), 16)
                elif kind == "small":
                    s = slot_sem(None)
                    sp.dma_start(wq, w_q_up[a].rearrange("(k p) n -> p k n", p=P)).then_inc(s, 16)
                    sp.dma_start(wkv, w_kv_up[a]).then_inc(s, 16)
                    for g, w in enumerate((w_a, w_x)):
                        pair = w[a].rearrange("(i two) r c -> two r i c", two=2)
                        for two in range(2):
                            r = slice(64 * two, 64 * two + 64)
                            sp.dma_start(wbd[r, g, :, r], pair[two]).then_inc(s, 16)
                elif kind == "ffn":
                    chunk(slot, ffn_gate[0], ffn_up[0], ffn_down[0], i * FW)
                else:
                    expert_chunk(slot, 0, i * FW)

            with sp.Fori(0, NE - 1) as e:
                for half in range(EH):
                    for s in range(SLOTS):
                        sp.wait_ge(sem("e_used"), e * ECHUNKS + half * SLOTS + s + 1)
                        if half == 0:
                            expert_chunk(s, e, (SLOTS + s) * FW)
                        else:
                            expert_chunk(s, e + 1, s * FW)
            for s in range(SLOTS):
                sp.wait_ge(sem("e_used"), (NE - 1) * ECHUNKS + s + 1)
                expert_chunk(s, NE - 1, (SLOTS + s) * FW)

            sp.wait_ge(sem("x_final"), 1)
            sp.dma_start(out[0].rearrange("(t p) d -> p t d", p=P), x[:, :, :]).then_inc(sem("out"), 16)
            sp.wait_ge(sem("out"), 16)

        @block.gpsimd
        def _(pool):
            g = nc.gpsimd
            g.memset(ident[:, :], 0.0).then_inc(sem("g0"), 1)
            g.memset(ones[:, :], 1.0).then_inc(sem("g0"), 1)
            g.memset(zero[:, :], 0.0).then_inc(sem("g0"), 1)
            g.memset(tri, 1.0).then_inc(sem("g0"), 1)
            g.memset(mask, 0.0).then_inc(sem("g0"), 1)
            for i, f in enumerate(inv_freq):
                g.memset(ivf[:, i:i + 1], f).then_inc(sem("g0"), 1)
            pool.wait_ge(sem("g0"), 5 + HALF)
            g.affine_select(out=ident[:, :], in_=ident[:, :], compare_op=ALU.not_equal, fill=1.0, base=0,
                            pattern=[[-1, P]], channel_multiplier=1).then_inc(sem("consts"), 1)
            g.affine_select(out=tri, in_=tri, compare_op=ALU.is_gt, fill=0.0, base=0,
                            pattern=[[1, P]], channel_multiplier=-1).then_inc(sem("consts"), 1)
            g.affine_select(out=mask[:, P:2 * P], in_=mask[:, P:2 * P], compare_op=ALU.is_ge, fill=NEG, base=0,
                            pattern=[[-1, P]], channel_multiplier=1).then_inc(sem("consts"), 1)
            g.iota(iota[:, :], pattern=[[1, SEQ]], base=0, channel_multiplier=0,
                   allow_small_or_imprecise_dtypes=True).then_inc(sem("consts"), 1)

            def ada(a):
                prev = None
                for i in range(4):
                    slot = wait_fill(pool, "ada", a, i)
                    w = ring[:, slot, :].rearrange("p (k n) -> p k n", k=2)
                    n = (a - 1) * 4 + i
                    for k in range(2):
                        g.tensor_scalar(w[:, k, :], w[:, k, :], cact[:, 2 * i + k:2 * i + k + 1], 0.0, ALU.mult,
                                        ALU.add).then_inc(sem("g_prod"), 1)
                    pool.wait_ge(sem("g_prod"), 2 * (n + 1))
                    if prev is not None:
                        g.tensor_tensor(w[:, 0, :], w[:, 0, :], prev, ALU.add).then_inc(sem("g_sum"), 1)
                        pool.wait_ge(sem("g_sum"), n - a + 1)
                    g.tensor_tensor(w[:, 0, :], w[:, 0, :], w[:, 1, :], ALU.add).then_inc(sem("ada_step1"), 1)
                    pool.wait_ge(sem("ada_step1"), n + 1)
                    prev = w[:, 0, :]

            for l in range(DEPTH):
                if l:
                    pool.wait_ge(sem("f_used"), CHUNKS)
                    pool.wait_ge(sem("xT_ps"), 3)
                else:
                    pool.wait_ge(sem("cols_in"), 1)
                    pool.wait_ge(sem("xT_ps"), 1)
                    pool.wait_ge(sem("setup"), 2)
                g.memset(wbd[:, 0, :, :], 0.0).then_inc(sem("g2"), 1)
                g.memset(wbd[:, 1, :, :], 0.0).then_inc(sem("g2"), 1)
                g.memset(xp[:, :, 0:TAPS - 1], 0.0).then_inc(sem("pad"), 1)
                pool.wait_ge(sem("g2"), 2 * (l + 1))
                pool.wait_ge(sem("pad"), l + 1)
                g.memset(mark[:, 0:1], 0.0).then_inc(sem("wbd_zero"), 1)
                ada(2 * l + 1)
                if l == 0:
                    ada(2)

        @block.tensor
        def _(pe):
            mm = nc.tensor.matmul
            tr = nc.tensor.transpose

            def ada_reduce(a):
                if a == 0:
                    pe.wait_ge(sem("ada_step0"), 4)
                else:
                    pe.wait_ge(sem("ada_step1"), 4 * a)
                acc = ring[:, landed["ada", a, 3][0], 0:3 * D]
                for j in range(3 * KD):
                    last = mm(ps[:, 4, j:j + 1], acc[:, j * P:(j + 1) * P], ones[:, 0:1], start=True, stop=True)
                last.then_inc(sem("ada_red"), 1)

            def norm_transposes(n):
                pe.wait_ge(sem("xn"), n + 1)
                for j in range(KD):
                    for t in range(NT):
                        last = tr(ps[:, j // 2, (j % 2) * SEQ + t * P:(j % 2) * SEQ + (t + 1) * P],
                                  xn[:, t, j * P:(j + 1) * P], ident[:, :])
                last.then_inc(sem("xT_ps"), 1)
                pe.wait_ge(sem("hT_act"), n + 1)
                pe.wait_ge(sem("hT_dve"), n + 1)

            def residual_transposes(n):
                pe.wait_ge(sem("yg"), n + 1)
                for t in range(NT):
                    for j in range(KD):
                        last = tr(ps[:, 2 * t + j // 4, (j % 4) * P:(j % 4 + 1) * P], ygT[:, j, t * P:(t + 1) * P],
                                  ident[:, :])
                last.then_inc(sem("res_ps"), 1)

            def mixer(l):
                ada_reduce(2 * l)
                norm_transposes(2 * l)
                halves = []
                for i in range(2):
                    slot = wait_fill(pe, "win", l, i)
                    halves.append(ring[:, slot, 0:4 * IN_COLS].rearrange("p (k n) -> p k n", k=4))

                def win(k, a, b):
                    return halves[k // 4][:, k % 4, a:b]

                for t in range(NT):
                    for k in range(KD):
                        last = mm(ps[:, 4 + t, 0:LAT], hT[:, k, t * P:(t + 1) * P], win(k, 0, LAT),
                                  start=(k == 0), stop=(k == KD - 1))
                    last.then_inc(sem("lat_ps"), 1)
                for part_, b0 in ((0, 6), (1, 0)):
                    for i in range(LT):
                        c0 = LAT + part_ * LRU + i * P
                        for k in range(KD):
                            last = mm(ps[:, b0 + i // 2, (i % 2) * SEQ:(i % 2 + 1) * SEQ], win(k, c0, c0 + P),
                                      hT[:, k, :], start=(k == 0), stop=(k == KD - 1))
                    last.then_inc(sem("rec_ps"), 1)
                last = mm(ps[:, 3, 0:1], ident[:, :], zero[:, 0:1], start=True, stop=True)
                last.then_inc(sem("z_done"), 1)
                pe.wait_ge(sem("cn"), l + 1)
                for i in range(3):
                    for t in range(NT):
                        last = tr(ps[:, 2 + i // 2, (i % 2) * SEQ + t * P:(i % 2) * SEQ + (t + 1) * P],
                                  cn[:, t, i * P:(i + 1) * P], ident[:, :])
                last.then_inc(sem("cT_ps"), 1)
                pe.wait_ge(sem("cT"), l + 1)
                wait_fill(pe, "small", l, 0)
                for t, (bq, bk) in enumerate(((4, 2), (6, 0))):
                    if t == 1:
                        pe.wait_ge(sem("rec_sb"), l + 1)
                    for half in range(2):
                        w = H * QK // 2
                        for k in range(2):
                            mm(ps[:, bq + half, 0:w], cT[:, k, t * P:(t + 1) * P], wq[:, k, half * w:(half + 1) * w],
                               start=(k == 0), stop=(k == 1))
                    for half in range(2):
                        last = mm(ps[:, bk + half, :], cT[:, 2, t * P:(t + 1) * P], wkv[:, half * 512:(half + 1) * 512],
                                  start=True, stop=True)
                    last.then_inc(sem("up_ps"), 1)
                for t, (bq, bk) in enumerate(((4, 2), (6, 0))):
                    pe.wait_ge(sem("qk"), 2 * l + t + 1)
                    pe.wait_ge(sem("v"), 2 * l + t + 1)
                    for src, b0 in ((qn, bq), (kn, bk)):
                        for h in range(H):
                            last = tr(ps[0:QK, b0 + h // 4, (h % 4) * P:(h % 4 + 1) * P], src[:, t, h, :], ident[:, :])
                    last.then_inc(sem("qkT_ps"), 1)
                pe.wait_ge(sem("qT"), 2 * l + 2)
                pe.wait_ge(sem("kT"), 2 * l + 2)
                for h in range(H):
                    last = mm(ps[:, 2 + h // 2, (h % 2) * SEQ:(h % 2 + 1) * SEQ], qT[0:QK, h, P:2 * P], kT[0:QK, h, :],
                              start=True, stop=True)
                last.then_inc(sem("s_ps"), 1)
                pe.wait_ge(sem("xr"), l + 1)
                for g, b0 in ((0, 6), (1, 0)):
                    for i in range(LT):
                        last = mm(ps[:, b0 + i // 2, (i % 2) * SEQ:(i % 2 + 1) * SEQ], wbd[:, g, i, :], lx[:, i, :],
                                  start=True, stop=True)
                last.then_inc(sem("rg_ps"), 1)
                pe.wait_ge(sem("rg"), l + 1)
                for h in range(H):
                    last = mm(ps[:, h // 4, (h % 4) * P:(h % 4 + 1) * P], qT[0:QK, h, 0:P], kT[0:QK, h, 0:P],
                              start=True, stop=True)
                last.then_inc(sem("s_ps"), 1)
                pe.wait_ge(sem("p"), 2 * l + 1)
                for kt in range(NT):
                    for h in range(H):
                        last = tr(ps[:, 2 + 2 * kt + h // 4, (h % 4) * P:(h % 4 + 1) * P],
                                  s1[:, h, kt * P:(kt + 1) * P], ident[:, :])
                last.then_inc(sem("pT_ps"), 1)
                pe.wait_ge(sem("p"), 2 * l + 2)
                for h in range(H):
                    last = tr(ps[:, h // 4, (h % 4) * P:(h % 4 + 1) * P], s0[:, h, :], ident[:, :])
                last.then_inc(sem("pT_ps"), 1)
                pe.wait_ge(sem("pT_a"), 2 * l + 1)
                pe.wait_ge(sem("pT_d"), l + 1)
                for h in range(H):
                    for kt in range(NT):
                        last = mm(ps[:, 7, h * V:(h + 1) * V], PT[:, 1 + kt, h, :], v_sb[:, kt, h * V:(h + 1) * V],
                                  start=(kt == 0), stop=(kt == NT - 1))
                last.then_inc(sem("o_ps"), 1)
                pe.wait_ge(sem("pT_a"), 2 * l + 2)
                for h in range(H):
                    last = mm(ps[:, 6, h * V:(h + 1) * V], PT[:, 0, h, :], v_sb[:, 0, h * V:(h + 1) * V],
                              start=True, stop=True)
                last.then_inc(sem("o_ps"), 1)
                pe.wait_ge(sem("recsq"), l + 1)
                for i in range(LT):
                    last = mm(ps[:, 2, 0:SEQ], ones[:, :], la[:, i, :], start=(i == 0), stop=(i == LT - 1))
                last.then_inc(sem("rss_ps"), 1)
                pe.wait_ge(sem("on"), l + 1)
                for i in range(LT):
                    for t in range(NT):
                        last = tr(ps[:, i // 2, (i % 2) * SEQ + t * P:(i % 2) * SEQ + (t + 1) * P],
                                  osb[:, t, 2 * i:2 * i + 2, :].rearrange("p a b -> p (a b)"), ident[:, :])
                last.then_inc(sem("onT_ps"), 1)
                pe.wait_ge(sem("mT"), l + 1)
                halves = []
                for i in range(2):
                    slot = wait_fill(pe, "wout", l, i)
                    halves.append(ring[:, slot, 0:4 * D].rearrange("p (k n) -> p k n", k=4))
                for j in range(KD):
                    for k in range(KD):
                        last = mm(ps[:, 4 + j // 2, (j % 2) * SEQ:(j % 2 + 1) * SEQ],
                                  halves[k // 4][:, k % 4, j * P:(j + 1) * P], mT[:, k, :],
                                  start=(k == 0), stop=(k == KD - 1))
                last.then_inc(sem("wout_done"), 1)
                residual_transposes(2 * l)

            def dense():
                ada_reduce(1)
                norm_transposes(1)

                def down(c):
                    _, _, wd = slot_parts(landed["ffn", 0, c][0])
                    pe.wait_ge(sem("f_hid"), c + 1)
                    for f in range(FT):
                        for j in range(KD):
                            last = mm(ps[:, 4 + j // 2, (j % 2) * SEQ:(j % 2 + 1) * SEQ], wd[:, f, j * P:(j + 1) * P],
                                      f_hid[:, c % 2, f, :], start=(c == 0 and f == 0 and j % 2 == 0),
                                      stop=(c == CHUNKS - 1 and f == FT - 1), skip_group_check=True)
                    last.then_inc(sem("f_used"), 1)

                for c in range(CHUNKS):
                    slot = wait_fill(pe, "ffn", 0, c)
                    wg, wu, _ = slot_parts(slot)
                    if c >= 2:
                        pe.wait_ge(sem("f_hid"), c - 1)
                    for w, b in ((wg, 0), (wu, 1)):
                        for f in range(FT):
                            for k in range(KD):
                                last = mm(ps[:, 2 * (c % 2) + b, f * SEQ:(f + 1) * SEQ], w[:, k, f * P:(f + 1) * P],
                                          hT[:, k, :], start=(k == 0), stop=(k == KD - 1))
                    last.then_inc(sem("f_gu"), 1)
                    if c:
                        down(c - 1)
                down(CHUNKS - 1)
                residual_transposes(1)

            def experts():
                ada_reduce(3)
                norm_transposes(3)
                pe.wait_ge(sem("consts"), 4)
                pe.wait_ge(sem("rw_in"), 16)
                for t in range(NT):
                    for k in range(KD):
                        last = mm(ps[:, 4, t * NE:(t + 1) * NE], hT[:, k, t * P:(t + 1) * P], rw[:, k, :],
                                  start=(k == 0), stop=(k == KD - 1))
                last.then_inc(sem("lg_ps"), 1)
                for t in range(NT):
                    for j in range(KD):
                        last = tr(ps[:, 2 * t + j // 4, (j % 4) * P:(j % 4 + 1) * P], hT[:, j, t * P:(t + 1) * P],
                                  ident[:, :])
                last.then_inc(sem("hnat_ps"), 1)
                pe.wait_ge(sem("chosen"), 1)
                mm(ps[:, 5, 0:NE], tri, rs[:, 0:NE], start=True, stop=True)
                mm(ps[:, 5, NE:2 * NE], ones[:, :], rs[:, 0:NE], start=True, stop=False)
                mm(ps[:, 5, NE:2 * NE], tri, rs[:, NE:2 * NE], start=False, stop=True)
                mm(ps[:, 6, 0:NE], ones[:, :], rs[:, 0:NE], start=True, stop=False)
                mm(ps[:, 6, 0:NE], ones[:, :], rs[:, NE:2 * NE], start=False, stop=True).then_inc(sem("rank_ps"), 1)
                pe.wait_ge(sem("hnat"), 2)
                pe.wait_ge(sem("meta"), 1)
                with pe.Fori(0, NE) as e:
                    n = pe.value_load(meta[0:1, bass.ds(e, 1)], min_val=1, max_val=NBLK)
                    cum = pe.value_load(meta[0:1, bass.ds(e + NE, 1)], min_val=0, max_val=NBLK * NE)
                    with pe.Fori(0, n) as b:
                        pe.wait_ge(sem("x_add"), cum)
                        pe.wait_ge(sem("sel"), cum + b + 1)
                        for k in range(KD):
                            for t in range(NT):
                                last = mm(ps[:, bass.ds(b, 1), k * BLK:(k + 1) * BLK], hnat[:, t, k * P:(k + 1) * P],
                                          sel[:, t, :], start=(t == 0), stop=(t == NT - 1), skip_group_check=True)
                        last.then_inc(sem("gath_ps"), 1)
                        mm(ps[:, bass.ds(b + 4, 1), 0:1], ident[:, :], zero[:, 0:1], start=True, stop=False,
                           skip_group_check=True)
                    def marker():
                        return mm(ps[:, 4, 0:1], ident[:, :], zero[:, 0:1], start=False, stop=False,
                                  skip_group_check=True)

                    with pe.Fori(0, EH) as half:
                        q0 = e * ECHUNKS + half * SLOTS

                        def down(s):
                            _, _, wd = slot_parts(s)
                            with pe.Fori(0, n) as b:
                                pe.wait_ge(sem("e_hid"), q0 + s + 1)
                                for f in range(FT):
                                    for j in range(KD):
                                        mm(ps[:, bass.ds(b + 4, 1), j * BLK:(j + 1) * BLK], wd[:, f, j * P:(j + 1) * P],
                                           e_hid[:, s % 2, bass.ds(b, 1), f * BLK:(f + 1) * BLK], start=False,
                                           stop=False, skip_group_check=True)
                            marker().then_inc(sem("e_used"), 1)

                        for s in range(SLOTS):
                            wg, wu, _ = slot_parts(s)
                            with pe.Fori(0, n) as b:
                                if s == 0:
                                    pe.wait_ge(sem("hTe"), cum + n)
                                pe.wait_ge(slot_sem(s), (2 * e + half + 1) * 48 + before_moe[s])
                                pe.wait_ge(sem("e_hid"), q0 + s)
                                for i, w in enumerate((wg, wu)):
                                    for f in range(FT):
                                        at = (i * FT + f) * BLK
                                        for k in range(KD):
                                            mm(ps[:, bass.ds(b, 1), at:at + BLK], w[:, k, f * P:(f + 1) * P],
                                               hT[:, k, bass.ds(b * BLK, BLK)], start=(k == 0),
                                               stop=(k == KD - 1), skip_group_check=True)
                            marker().then_inc(sem("e_gu"), 1)
                            if s:
                                down(s - 1)
                        down(SLOTS - 1)

                    with pe.Fori(0, n) as b:
                        done = cum + b
                        pe.wait_ge(sem("x_add"), done)
                        pe.wait_ge(sem("sw"), done + 1)
                        mm(ps[:, 2, 0:1], ident[:, :], zero[:, 0:1], start=True, stop=True)
                        for t in range(NT):
                            tr(ps[0:BLK, 2, t * P:(t + 1) * P], sel[:, t, :], ident[:, :])
                        pe.wait_ge(sem("yT"), done + 1)
                        mm(ps[:, 0, 0:1], ident[:, :], zero[:, 0:1], start=True, stop=True)
                        for j in range(KD):
                            last = tr(ps[0:BLK, j // 4, (j % 4) * P:(j % 4 + 1) * P], yT[:, j, :], ident[:, :])
                        last.then_inc(sem("y_ps"), 1)
                        pe.wait_ge(sem("y_sb"), done + 1)
                        for i, bank in enumerate((3, 0, 1, 2)):
                            t, half = i // 2, i % 2
                            last = mm(ps[:, bank, :], swT[0:BLK, t * P:(t + 1) * P],
                                      ynat[0:BLK, half * 512:(half + 1) * 512], start=True, stop=True)
                        last.then_inc(sem("spread_ps"), 1)

            pe.wait_ge(sem("consts"), 1)
            pe.wait_ge(sem("rowsA_in"), 16 * 9)
            pe.wait_ge(sem("rowsB_in"), 16)
            tr(ps[:, 0, 0:126], rowsA[0:126, :], ident[0:126, 0:126])
            tr(ps[:, 0, P:P + 96], rowsB[0:96, :], ident[0:96, 0:96]).then_inc(sem("cols_ps"), 1)
            pe.wait_ge(sem("cols_in"), 1)
            for l in range(DEPTH):
                mixer(l)
                if l == 0:
                    dense()
                else:
                    experts()

        @block.scalar
        def _(act):
            A = nc.scalar.activation
            r = rowsA
            s = sem("rowsA_in")
            act.dma_start(r[C0:C0 + 8, :], c_in[0].rearrange("(j p) -> j p", p=P)).then_inc(s, 16)
            act.dma_start(r[NG:NG + 32, :], norm_gain.rearrange("l s (j p) -> (l s j) p", p=P)).then_inc(s, 16)
            act.dma_start(rowsB[0:96, :], b_ada.rearrange("l s (j p) -> (l s j) p", p=P)).then_inc(sem("rowsB_in"), 16)
            act.dma_start(r[OG:OG + 16, :], out_gain.rearrange("l (j p) -> (l j) p", p=P)).then_inc(s, 16)
            act.dma_start(r[LG:LG + 6, :], latent_gain.rearrange("l (j p) -> (l j) p", p=P)).then_inc(s, 16)
            act.dma_start(r[CW:CW + 32, :], conv_w.rearrange("l w (j p) -> (l w j) p", p=P)).then_inc(s, 16)
            for at, v in ((CB, conv_b), (BA, b_a), (BX, b_x), (LM, lru_lambda)):
                act.dma_start(r[at:at + 8, :], v.rearrange("l (j p) -> (l j) p", p=P)).then_inc(s, 16)
            act.dma_start(pos_i[:, :], pos_in[0].rearrange("(t p) -> p t", p=P),
                          allow_slow_non_contiguous=True).then_inc(sem("pos_in"), 16)
            for l in range(DEPTH):
                for i, v in enumerate((q_gain, k_gain)):
                    act.dma_start(gains[:, 2 * l + i, :], v[l:l + 1, :].partition_broadcast(P)
                                  if False else v[l:l + 1, :].broadcast_to([P, QK])).then_inc(sem("gains_in"), 16)
            act.dma_start(rw, router_w[0].rearrange("(k p) e -> p k e", p=P)).then_inc(sem("rw_in"), 16)

            act.wait_ge(sem("cols_in"), 1)
            A(cact[:, :], colA[:, C0:C0 + KD], ACT.Tanh, scale=0.5).then_inc(sem("a_set"), 1)
            A(m2ls[:, :], colA[:, LM:LM + 8], ACT.Abs).then_inc(sem("a_set"), 1)
            act.wait_ge(sem("a_set"), 2)
            A(m2ls[:, :], m2ls[:, :], ACT.Exp, scale=-1.0).then_inc(sem("a_set"), 1)
            act.wait_ge(sem("ang"), 1)
            A(cs.rearrange("p t i n -> p i t n"), ang, ACT.Sin).then_inc(sem("cs"), 1)

            roots = [0]

            def root(n):
                roots[0] += 1
                act.wait_ge(sem("ms"), roots[0])
                A(rs[:, 0:n], st[:, 0:n], ACT.Sqrt).then_inc(sem("root"), 1)

            def norm(n):
                if n == 0:
                    act.wait_ge(sem("x_in"), 16)
                else:
                    act.wait_ge(sem("x_new"), n)
                for t in range(NT):
                    A(xn[:, t, :], x[:, t, :], ACT.Square, accum_out=st[:, t:t + 1]).then_inc(sem("ss_n"), 1)
                root(NT)
                act.wait_ge(sem("xT_ps"), n + 1)
                act.wait_ge(sem("mod"), n + 1)
                for j in range(KD // 2):
                    last = A(hT[:, j, :], ps[:, j // 2, (j % 2) * SEQ:(j % 2 + 1) * SEQ], ACT.Identity,
                             bias=adav[:, n, j:j + 1], scale=adaA[:, n, j:j + 1])
                last.then_inc(sem("hT_act"), 1)

            def gate_evac(n):
                for j in range(KD // 2):
                    last = A(ygT[:, j, :], ps[:, 4 + j // 2, (j % 2) * SEQ:(j % 2 + 1) * SEQ], ACT.Copy,
                             scale=adav[:, n, 16 + j:17 + j])
                last.then_inc(sem("yg"), 1) if False else last.then_inc(sem("yg_a"), 1)

            def mixer(l):
                norm(2 * l)
                for t in range(NT):
                    act.wait_ge(sem("lat_ps"), 2 * l + t + 1)
                    for i, (a, b) in enumerate(((0, Q_RANK), (Q_RANK, Q_RANK + KV_RANK), (Q_RANK + KV_RANK, LAT))):
                        last = A(cn[:, t, a:b], ps[:, 4 + t, a:b], ACT.Square, accum_out=st[:, 3 * t + i:3 * t + i + 1])
                last.then_inc(sem("ss_l"), 1)
                root(3 * NT)
                act.wait_ge(sem("pad"), l + 1)
                act.wait_ge(sem("rec_ps"), 2 * l + 1)
                A(xp[:, :, TAPS - 1:], bank2(6).rearrange("p (i n) -> p i n", i=LT), ACT.Copy).then_inc(sem("xp"), 1)
                act.wait_ge(sem("rec_ps"), 2 * l + 2)
                A(gr, bank2(0).rearrange("p (i n) -> p i n", i=LT), ACT.Copy).then_inc(sem("rec_sb"), 1)
                act.wait_ge(sem("rec_sb"), l + 1)
                A(lq, gr, ACT.Square).then_inc(sem("g_sq"), 1)
                for t, (bq, bk) in enumerate(((4, 2), (6, 0))):
                    act.wait_ge(sem("up_ps"), 2 * l + t + 1)
                    if t or l:
                        act.wait_ge(sem("sq_used"), 2 * (2 * l + t))
                    else:
                        act.wait_ge(sem("cT_ps"), 1)
                    for half in range(2):
                        A(sq[:, half * 384:(half + 1) * 384], ps[:, bq + half, 0:384], ACT.Square)\
                            .then_inc(sem("q_sq"), 1)
                    act.wait_ge(sem("sq_used"), 2 * (2 * l + t) + 1)
                    for half in range(2):
                        kvb = ps[:, bk + half, :].rearrange("p (h n) -> p h n", h=H // 2)
                        A(sq[:, half * 256:(half + 1) * 256].rearrange("p (h n) -> p h n", h=H // 2),
                          kvb[:, :, 0:NOPE], ACT.Square).then_inc(sem("k_sq"), 1)
                    for half in range(2):
                        kvb = ps[:, bk + half, :].rearrange("p (h n) -> p h n", h=H // 2)
                        last = A(v_sb[:, t, half * 256:(half + 1) * 256].rearrange("p (h n) -> p h n", h=H // 2),
                                 kvb[:, :, NOPE:NOPE + V], ACT.Copy)
                    last.then_inc(sem("v"), 1)
                    root(24)
                act.wait_ge(sem("g_arg"), l + 1)
                A(lq, lq, ACT.Tanh, scale=GELU_B).then_inc(sem("g_tanh"), 1)
                for t, bq in enumerate((4, 6)):
                    act.wait_ge(sem("qkT_ps"), 2 * l + t + 1)
                    for half in range(2):
                        last = A(qT[0:QK, 4 * half:4 * half + 4, t * P:(t + 1) * P],
                                 ps[0:QK, bq + half, :].rearrange("p (h n) -> p h n", h=4), ACT.Copy)
                    last.then_inc(sem("qT"), 1)
                act.wait_ge(sem("rg_ps"), l + 1)
                for g, (b0, dst) in enumerate(((6, la), (0, li))):
                    for i in range(LT):
                        last = A(dst[:, i, :], ps[:, b0 + i // 2, (i % 2) * SEQ:(i % 2 + 1) * SEQ], ACT.Tanh,
                                 bias=hb[:, g * 8 + l * LT + i:g * 8 + l * LT + i + 1], scale=0.5)
                last.then_inc(sem("rg"), 1)
                act.wait_ge(sem("rg"), l + 1)
                for i in range(LT):
                    m = m2ls[:, l * LT + i:l * LT + i + 1]
                    last = A(la[:, i, :], la[:, i, :], ACT.Tanh, bias=m, scale=m)
                last.then_inc(sem("lt"), 1)
                for n, (buf, keys) in enumerate(((s1, SEQ), (s0, P))):
                    act.wait_ge(sem("nmax"), 2 * l + n + 1)
                    for h in range(H):
                        last = A(buf[:, h, :], buf[:, h, :], ACT.Exp, bias=mx[:, n * H + h:n * H + h + 1],
                                 scale=SCALE, accum_out=den[:, n * H + h:n * H + h + 1])
                    last.then_inc(sem("p"), 1)
                act.wait_ge(sem("pT_ps"), 2 * l + 1)
                A(PT[:, 1, :, :].rearrange("p h n -> p (h n)"), bank2(2), ACT.Copy).then_inc(sem("pT_a"), 1)
                act.wait_ge(sem("pT_ps"), 2 * l + 2)
                A(PT[:, 0, :, :].rearrange("p h n -> p (h n)"), bank2(0), ACT.Copy).then_inc(sem("pT_a"), 1)
                act.wait_ge(sem("lq_free"), l + 1)
                A(lq, la, ACT.Sqrt).then_inc(sem("lroot"), 1)
                act.wait_ge(sem("rec"), l + 1)
                A(la, lx, ACT.Square).then_inc(sem("recsq"), 1)
                act.wait_ge(sem("o_sb"), l + 1)
                for t in range(NT):
                    last = A(PT[:, t, 0:H // 2, :].rearrange("p h n -> p (h n)"),
                             osb[:, t, :, :].rearrange("p h n -> p (h n)"), ACT.Square,
                             accum_out=st[:, t:t + 1])
                last.then_inc(sem("ss_o"), 1)
                root(NT)
                act.wait_ge(sem("rbc_ms"), l + 1)
                A(rbc, rbc, ACT.Sqrt).then_inc(sem("rbc_root"), 1)
                act.wait_ge(sem("onT_ps"), l + 1)
                for i in range(2):
                    last = A(mT[:, i, :], ps[:, 0, i * SEQ:(i + 1) * SEQ], ACT.Copy,
                             scale=colA[:, OG + 8 * l + i:OG + 8 * l + i + 1])
                last.then_inc(sem("mT_a"), 1)
                act.wait_ge(sem("wout_done"), l + 1)
                gate_evac(2 * l)

            def dense():
                norm(1)
                for c in range(CHUNKS):
                    act.wait_ge(sem("f_gu"), c + 1)
                    if c:
                        act.wait_ge(sem("f_hid"), c)
                    A(f_tg.rearrange("p f n -> p (f n)"), ps[:, 2 * (c % 2), :], ACT.Tanh, scale=0.5)\
                        .then_inc(sem("f_tanh"), 1)
                act.wait_ge(sem("f_used"), CHUNKS)
                gate_evac(1)

            def experts():
                norm(3)
                act.wait_ge(sem("hnat_ps"), 1)
                A(hnat[:, 0, :], bank2(0), ACT.Copy).then_inc(sem("hnat"), 1)
                act.wait_ge(sem("w_dif"), 1)
                A(st[:, 8:10], st[:, 8:10], ACT.Exp).then_inc(sem("w_exp"), 1)
                act.wait_ge(sem("meta"), 1)
                with act.Fori(0, NE) as e:
                    n = act.value_load(meta[0:1, bass.ds(e, 1)], min_val=1, max_val=NBLK)
                    cum = act.value_load(meta[0:1, bass.ds(e + NE, 1)], min_val=0, max_val=NBLK * NE)
                    with act.Fori(0, n) as b:
                        act.wait_ge(sem("gath_ps"), cum + b + 1)
                        A(hT[:, :, bass.ds(b * BLK, BLK)],
                          ps[:, bass.ds(b, 1), :].rearrange("p b (k n) -> p (b k) n", k=KD), ACT.Copy)\
                            .then_inc(sem("hTe"), 1)
                    with act.Fori(0, EH) as half:
                        q0 = e * ECHUNKS + half * SLOTS
                        for s_ in range(SLOTS):
                            act.wait_ge(sem("e_gu"), q0 + s_ + 1)
                            with act.Fori(0, n) as b:
                                A(e_tg[:, bass.ds(b, 1), :], ps[:, bass.ds(b, 1), 0:FT * BLK], ACT.Tanh, scale=0.5)
                            A(mark[:, 1:2], zero[:, 0:1], ACT.Copy).then_inc(sem("e_tanh"), 1)
                    with act.Fori(0, n) as b:
                        act.wait_ge(sem("y_ps"), cum + b + 1)
                        A(swT[0:BLK, :], ps[0:BLK, 2, 0:NT * P], ACT.Copy)
                        A(ynat[0:BLK, :], ps[0:BLK, 0:2, :].rearrange("p b n -> p (b n)"), ACT.Copy)\
                            .then_inc(sem("y_sb"), 1)

            for l in range(DEPTH):
                mixer(l)
                if l == 0:
                    dense()
                else:
                    experts()

        @block.vector
        def _(dve):
            v = nc.vector
            chain = [0]

            def link(ins):
                chain[0] += 1
                ins.then_inc(sem("dve"), 1)
                dve.wait_ge(sem("dve"), chain[0])

            roots = [0]

            def rstd(n, inv):
                roots[0] += 1
                v.tensor_scalar(st[:, 0:n], st[:, 0:n], inv, EPS, ALU.mult, ALU.add).then_inc(sem("ms"), 1)
                dve.wait_ge(sem("root"), roots[0])
                link(v.reciprocal(rs[:, 0:n], rs[:, 0:n]))

            dve.wait_ge(sem("cols_ps"), 1)
            v.tensor_copy(colA[:, :], ps[:, 0, 0:126])
            v.tensor_copy(colB[:, :], ps[:, 0, P:P + 96]).then_inc(sem("cols_in"), 1)
            dve.wait_ge(sem("cols_in"), 1)
            link(v.tensor_scalar(hb[:, :], colA[:, BA:BA + 16], 0.5, None, ALU.mult))
            dve.wait_ge(sem("a_set"), 3)
            link(v.tensor_scalar(cact[:, :], cact[:, :], 0.5, 0.5, ALU.mult, ALU.add))
            link(v.tensor_tensor(cact[:, :], cact[:, :], colA[:, C0:C0 + KD], ALU.mult))
            v.tensor_copy(mark[:, 4:5], cact[:, 0:1]).then_inc(sem("setup"), 1)

            prev = None
            for i in range(4):
                slot = wait_fill(dve, "ada", 0, i)
                w = ring[:, slot, :].rearrange("p (k n) -> p k n", k=2)
                if prev is None:
                    link(v.tensor_scalar(w[:, 0, :], w[:, 0, :], cact[:, 0:1], None, ALU.mult))
                else:
                    link(v.scalar_tensor_tensor(out=w[:, 0, :], in0=w[:, 0, :], scalar=cact[:, 2 * i:2 * i + 1],
                                                in1=prev, op0=ALU.mult, op1=ALU.add))
                v.scalar_tensor_tensor(out=w[:, 0, :], in0=w[:, 1, :], scalar=cact[:, 2 * i + 1:2 * i + 2],
                                       in1=w[:, 0, :], op0=ALU.mult, op1=ALU.add).then_inc(sem("ada_step0"), 1)
                dve.wait_ge(sem("ada_step0"), i + 1)
                prev = w[:, 0, :]
                if i == 0:
                    z, z2, pz = st[:, 0:8], st[:, 8:16], st[:, 16:24]
                    link(v.tensor_scalar(z, m2ls[:, :], 2.0, None, ALU.add))
                    link(v.reciprocal(z, z))
                    link(v.tensor_tensor(z, z, m2ls[:, :], ALU.mult))
                    link(v.tensor_tensor(z2, z, z, ALU.mult))
                    link(v.tensor_scalar(pz, z2, 1.0 / 17.0, None, ALU.mult))
                    for k in range(7, 0, -1):
                        link(v.scalar_tensor_tensor(out=pz, in0=pz, scalar=1.0 / (2 * k + 1), in1=z2, op0=ALU.add,
                                                    op1=ALU.mult))
                    link(v.scalar_tensor_tensor(out=pz, in0=pz, scalar=1.0, in1=z, op0=ALU.add, op1=ALU.mult))
                    link(v.tensor_scalar(z, colA[:, LM:LM + 8], 0.0, -2.0, ALU.min, ALU.mult))
                    link(v.scalar_tensor_tensor(out=m2ls[:, :], in0=pz, scalar=4.0, in1=z, op0=ALU.mult, op1=ALU.add))
                if i == 1:
                    c1, c2, c3 = cody_waite()
                    dve.wait_ge(sem("pos_in"), 16)
                    dve.wait_ge(sem("consts"), 4)
                    link(v.tensor_copy(pos_f[:, :], pos_i[:, :]))
                    for j in range(2):
                        for t in range(NT):
                            link(v.tensor_scalar(ang[:, j, t, :], ivf, pos_f[:, t:t + 1], None, ALU.mult))
                        magic = 1.5 * 2.0 ** 23
                        link(v.tensor_scalar(angk[:, j, :, :], ang[:, j, :, :], 1.0 / TWO_PI, 0.25 if j == 0 else 0.0,
                                             ALU.mult, ALU.add))
                        link(v.tensor_scalar(angk[:, j, :, :], angk[:, j, :, :], magic, None, ALU.add))
                        link(v.tensor_scalar(angk[:, j, :, :], angk[:, j, :, :], -magic, None, ALU.add))
                        for c in (c1, c2, c3):
                            link(v.scalar_tensor_tensor(out=ang[:, j, :, :], in0=angk[:, j, :, :], scalar=-c,
                                                        in1=ang[:, j, :, :], op0=ALU.mult, op1=ALU.add))
                        if j == 0:
                            link(v.tensor_scalar(ang[:, j, :, :], ang[:, j, :, :], float(np.pi / 2), None, ALU.add))
                        link(v.tensor_scalar(ang[:, j, :, :], ang[:, j, :, :], -3.1415925, 3.1415925, ALU.max, ALU.min))
                    v.tensor_copy(mark[:, 5:6], cact[:, 0:1]).then_inc(sem("ang"), 1)
                if i == 2:
                    dve.wait_ge(sem("cs"), 1)
                    v.tensor_copy(mark[:, 6:7], cact[:, 0:1]).then_inc(sem("setup"), 1)

            def norm(n):
                dve.wait_ge(sem("ada_red"), n + 1)
                link(v.tensor_tensor(adav[:, n, :], ps[:, 4, 0:24], colB[:, 24 * n:24 * n + 24], ALU.add))
                v.scalar_tensor_tensor(out=adaA[:, n, :], in0=adav[:, n, 8:16], scalar=1.0,
                                       in1=colA[:, NG + 8 * n:NG + 8 * n + 8], op0=ALU.add, op1=ALU.mult)\
                    .then_inc(sem("mod"), 1)
                dve.wait_ge(sem("ss_n"), 2 * (n + 1))
                rstd(NT, 1.0 / D)
                if n == 0:
                    dve.wait_ge(sem("x_in"), 16)
                for t in range(NT):
                    last = v.tensor_scalar(xn[:, t, :], x[:, t, :], rs[:, t:t + 1], None, ALU.mult)
                last.then_inc(sem("xn"), 1)
                dve.wait_ge(sem("xT_ps"), n + 1)
                dve.wait_ge(sem("mod"), n + 1)
                for j in range(KD // 2, KD):
                    last = v.tensor_scalar(hT[:, j, :], ps[:, j // 2, (j % 2) * SEQ:(j % 2 + 1) * SEQ],
                                           adaA[:, n, j:j + 1], adav[:, n, j:j + 1], ALU.mult, ALU.add)
                last.then_inc(sem("hT_dve"), 1)

            def residual(n):
                for j in range(KD // 2, KD):
                    last = v.tensor_scalar(ygT[:, j, :], ps[:, 4 + j // 2, (j % 2) * SEQ:(j % 2 + 1) * SEQ],
                                           adav[:, n, 16 + j:17 + j], None, ALU.mult)
                link(last)
                dve.wait_ge(sem("yg_a"), n + 1)
                v.tensor_copy(mark[:, 7:8], cact[:, 0:1]).then_inc(sem("yg"), 1)
                dve.wait_ge(sem("res_ps"), n + 1)
                for t in range(NT):
                    last = v.tensor_tensor(x[:, t, :], x[:, t, :], bank2(2 * t), ALU.add)
                last.then_inc(sem("x_new"), 1)
                dve.wait_ge(sem("x_new"), n + 1)

            def bc(col, n):
                return col.unsqueeze(2).broadcast_to([P, col.shape[1], n])

            def rope(dst, src, l, t, heads, n):
                cos = cs[:, t, 0:1, :].broadcast_to([P, heads, HALF])
                sin = cs[:, t, 1:2, :].broadcast_to([P, heads, HALF])
                x1, x2 = src[:, :, 0:HALF], src[:, :, HALF:ROPE]
                tmp = [rope_tmp[:, i, 0:heads, :] for i in range(4)]
                v.tensor_tensor(tmp[0], x1, cos, ALU.mult)
                v.tensor_tensor(tmp[1], x2, sin, ALU.mult)
                v.tensor_tensor(tmp[2], x1, sin, ALU.mult)
                link(v.tensor_tensor(tmp[3], x2, cos, ALU.mult))
                v.tensor_tensor(dst[:, :, 0:HALF], tmp[0], tmp[1], ALU.subtract)
                link(v.tensor_tensor(dst[:, :, HALF:ROPE], tmp[2], tmp[3], ALU.add))

            def mixer(l):
                norm(2 * l)
                dve.wait_ge(sem("ss_l"), l + 1)
                for t in range(NT):
                    for i, w in enumerate((Q_RANK, KV_RANK, ROPE)):
                        c = 3 * t + i
                        last = v.tensor_scalar(st[:, c:c + 1], st[:, c:c + 1], 1.0 / w, EPS, ALU.mult, ALU.add)
                roots[0] += 1
                last.then_inc(sem("ms"), 1)
                dve.wait_ge(sem("root"), roots[0])
                link(v.reciprocal(rs[:, 0:6], rs[:, 0:6]))
                for t in range(NT):
                    for i, (a, b) in enumerate(((0, Q_RANK), (Q_RANK, Q_RANK + KV_RANK), (Q_RANK + KV_RANK, LAT))):
                        last = v.tensor_scalar(cn[:, t, a:b], ps[:, 4 + t, a:b], rs[:, 3 * t + i:3 * t + i + 1], None,
                                               ALU.mult)
                last.then_inc(sem("cn"), 1)
                dve.wait_ge(sem("cn"), l + 1)
                if l == 0:
                    dve.wait_ge(sem("gains_in"), 64)
                for t in range(NT):
                    kr = cn[:, t, Q_RANK + KV_RANK:LAT]
                    link(v.tensor_tensor(kr, kr, gains[:, 2 * l + 1, NOPE:QK], ALU.mult))
                    rope(kn[:, t, 0:1, NOPE:QK], kr.unsqueeze(1), l, t, 1, 0)
                    v.tensor_copy(kn[:, t, 1:H, NOPE:QK], kn[:, t, 0:1, NOPE:QK].broadcast_to([P, H - 1, ROPE]))
                dve.wait_ge(sem("cT_ps"), l + 1)
                for i in range(3):
                    last = v.tensor_scalar(cT[:, i, :], ps[:, 2 + i // 2, (i % 2) * SEQ:(i % 2 + 1) * SEQ],
                                           colA[:, LG + 3 * l + i:LG + 3 * l + i + 1], None, ALU.mult)
                last.then_inc(sem("cT"), 1)
                dve.wait_ge(sem("xp"), l + 1)
                for w in range(TAPS):
                    for i in range(LT):
                        col = colA[:, CW + 16 * l + 4 * w + i:CW + 16 * l + 4 * w + i + 1]
                        src = xp[:, i, w:w + SEQ]
                        if w == 0:
                            last = v.tensor_scalar(lx[:, i, :], src, col, colA[:, CB + 4 * l + i:CB + 4 * l + i + 1],
                                                   ALU.mult, ALU.add)
                        else:
                            last = v.scalar_tensor_tensor(out=lx[:, i, :], in0=src, scalar=col, in1=lx[:, i, :],
                                                          op0=ALU.mult, op1=ALU.add)
                    if w < TAPS - 1:
                        link(last)
                last.then_inc(sem("xr"), 1)
                dve.wait_ge(sem("xr"), l + 1)
                for t, (bq, bk) in enumerate(((4, 2), (6, 0))):
                    n = 2 * l + t
                    dve.wait_ge(sem("q_sq"), 2 * (n + 1))
                    sqq = sq[:, 0:H * QK].rearrange("p (h n) -> p h n", h=H)
                    v.tensor_reduce(st[:, 0:H], sqq[:, :, 0:NOPE], AX, ALU.add)
                    v.tensor_reduce(st[:, H:2 * H], sqq[:, :, NOPE:QK], AX, ALU.add).then_inc(sem("sq_used"), 1)
                    dve.wait_ge(sem("k_sq"), 2 * (n + 1))
                    v.tensor_reduce(st[:, 2 * H:3 * H], sq[:, 0:H * NOPE].rearrange("p (h n) -> p h n", h=H), AX,
                                    ALU.add).then_inc(sem("sq_used"), 1)
                    dve.wait_ge(sem("sq_used"), 2 * (n + 1))
                    link(v.tensor_scalar(st[:, H:2 * H], st[:, H:2 * H], float(NOPE) / ROPE, None, ALU.mult))
                    rstd(3 * H, 1.0 / NOPE)
                    dve.wait_ge(sem("v"), n + 1)
                    for half in range(2):
                        hs = slice(4 * half, 4 * half + 4)
                        qb = ps[:, bq + half, 0:4 * QK].rearrange("p (h n) -> p h n", h=4)
                        kb = ps[:, bk + half, :].rearrange("p (h n) -> p h n", h=4)
                        v.tensor_tensor(qn[:, t, hs, 0:NOPE], qb[:, :, 0:NOPE],
                                        bc(rs[:, 4 * half:4 * half + 4], NOPE), ALU.mult)
                        v.tensor_tensor(qn[:, t, hs, NOPE:QK], qb[:, :, NOPE:QK],
                                        bc(rs[:, H + 4 * half:H + 4 * half + 4], ROPE), ALU.mult)
                        last = v.tensor_tensor(kn[:, t, hs, 0:NOPE], kb[:, :, 0:NOPE],
                                               bc(rs[:, 2 * H + 4 * half:2 * H + 4 * half + 4], NOPE), ALU.mult)
                    link(last)
                    link(v.tensor_tensor(qn[:, t, :, :], qn[:, t, :, :],
                                         gains[:, 2 * l:2 * l + 1, :].broadcast_to([P, H, QK]), ALU.mult))
                    v.tensor_tensor(kn[:, t, :, 0:NOPE], kn[:, t, :, 0:NOPE],
                                    gains[:, 2 * l + 1:2 * l + 2, 0:NOPE].broadcast_to([P, H, NOPE]), ALU.mult)
                    rope(qn[:, t, :, NOPE:QK], qn[:, t, :, NOPE:QK], l, t, H, 0)
                    v.tensor_copy(mark[:, 8:9], cact[:, 0:1]).then_inc(sem("qk"), 1)
                    if t == 0:
                        dve.wait_ge(sem("g_sq"), l + 1)
                        link(v.tensor_scalar(lq, lq, GELU_A, 1.0, ALU.mult, ALU.add))
                        v.tensor_tensor(lq, lq, gr, ALU.mult).then_inc(sem("g_arg"), 1)
                for t, bk in enumerate((2, 0)):
                    dve.wait_ge(sem("qkT_ps"), 2 * l + t + 1)
                    for half in range(2):
                        last = v.tensor_copy(kT[0:QK, 4 * half:4 * half + 4, t * P:(t + 1) * P],
                                             ps[0:QK, bk + half, :].rearrange("p (h n) -> p h n", h=4))
                    last.then_inc(sem("kT"), 1)
                dve.wait_ge(sem("g_tanh"), l + 1)
                v.scalar_tensor_tensor(out=gr, in0=lq, scalar=1.0, in1=gr, op0=ALU.add, op1=ALU.mult)\
                    .then_inc(sem("lq_free"), 1)
                for n, (buf, keys, b0, nb) in enumerate(((s1, SEQ, 2, 4), (s0, P, 0, 2))):
                    dve.wait_ge(sem("s_ps"), 2 * l + n + 1)
                    m = mask[:, SEQ - keys:SEQ].unsqueeze(1).broadcast_to([P, H, keys])
                    link(v.tensor_tensor(buf, bank2(b0, nb).rearrange("p (h n) -> p h n", h=H), m, ALU.add))
                    link(v.tensor_reduce(mx[:, n * H:(n + 1) * H], buf, AX, ALU.max))
                    v.tensor_scalar(mx[:, n * H:(n + 1) * H], mx[:, n * H:(n + 1) * H], -SCALE, None, ALU.mult)\
                        .then_inc(sem("nmax"), 1)
                dve.wait_ge(sem("lt"), l + 1)
                link(v.scalar_tensor_tensor(out=li, in0=li, scalar=1.0, in1=lx, op0=ALU.add, op1=ALU.mult))
                link(v.tensor_scalar(lr, la, 1.0, None, ALU.add))
                link(v.reciprocal(lr, lr))
                dve.wait_ge(sem("pT_ps"), 2 * l + 1)
                v.tensor_copy(PT[:, 2, :, :].rearrange("p h n -> p (h n)"), bank2(4)).then_inc(sem("pT_d"), 1)
                dve.wait_ge(sem("lroot"), l + 1)
                link(v.tensor_tensor(li, li, lr, ALU.mult))
                link(v.tensor_tensor(li, li, lq, ALU.mult))
                link(v.tensor_scalar(la, la, -1.0, 1.0, ALU.mult, ALU.add))
                link(v.tensor_tensor(la, la, lr, ALU.mult))
                for i in range(LT):
                    last = v.tensor_tensor_scan(lq[:, i, :], la[:, i, :], li[:, i, :], 0.0, ALU.mult, ALU.add)
                link(last)
                v.scalar_tensor_tensor(out=lx, in0=lq, scalar=0.5, in1=gr, op0=ALU.mult, op1=ALU.mult)\
                    .then_inc(sem("rec"), 1)
                link(v.reciprocal(den[:, :], den[:, :]))
                for n, t in enumerate((1, 0)):
                    dve.wait_ge(sem("o_ps"), 2 * l + n + 1)
                    last = v.tensor_tensor(osb[:, t, :, :], ps[:, 6 + t, :].rearrange("p (h n) -> p h n", h=H),
                                           bc(den[:, n * H:(n + 1) * H], V), ALU.mult)
                last.then_inc(sem("o_sb"), 1)
                dve.wait_ge(sem("ss_o"), l + 1)
                rstd(NT, 1.0 / (H * V))
                for t in range(NT):
                    o = osb[:, t, :, :].rearrange("p h n -> p (h n)")
                    last = v.tensor_scalar(o, o, rs[:, t:t + 1], None, ALU.mult)
                last.then_inc(sem("on"), 1)
                dve.wait_ge(sem("rss_ps"), l + 1)
                v.tensor_scalar(rbc, ps[:, 2, 0:SEQ], 1.0 / LRU, EPS, ALU.mult, ALU.add).then_inc(sem("rbc_ms"), 1)
                dve.wait_ge(sem("rbc_root"), l + 1)
                link(v.reciprocal(rbc, rbc))
                for i in range(LT):
                    v.scalar_tensor_tensor(out=mT[:, LT + i, :], in0=lx[:, i, :],
                                           scalar=colA[:, OG + 8 * l + LT + i:OG + 8 * l + LT + i + 1], in1=rbc,
                                           op0=ALU.mult, op1=ALU.mult)
                dve.wait_ge(sem("onT_ps"), l + 1)
                for i in range(2, LT):
                    last = v.tensor_scalar(mT[:, i, :], ps[:, 1, (i - 2) * SEQ:(i - 1) * SEQ],
                                           colA[:, OG + 8 * l + i:OG + 8 * l + i + 1], None, ALU.mult)
                link(last)
                dve.wait_ge(sem("mT_a"), l + 1)
                v.tensor_copy(mark[:, 9:10], cact[:, 0:1]).then_inc(sem("mT"), 1)
                dve.wait_ge(sem("wout_done"), l + 1)
                residual(2 * l)

            def dense():
                norm(1)
                for c in range(CHUNKS):
                    dve.wait_ge(sem("f_tanh"), c + 1)
                    b = 2 * (c % 2)
                    tg = f_tg.rearrange("p f n -> p (f n)")
                    link(v.scalar_tensor_tensor(out=tg, in0=tg, scalar=1.0, in1=ps[:, b, :], op0=ALU.add, op1=ALU.mult))
                    v.scalar_tensor_tensor(out=f_hid[:, c % 2, :, :].rearrange("p f n -> p (f n)"), in0=tg,
                                           scalar=0.5, in1=ps[:, b + 1, :], op0=ALU.mult, op1=ALU.mult)\
                        .then_inc(sem("f_hid"), 1)
                dve.wait_ge(sem("f_used"), CHUNKS)
                residual(1)

            def experts():
                norm(3)
                dve.wait_ge(sem("lg_ps"), 1)
                lg = st[:, 16:32]
                link(v.tensor_copy(lg, ps[:, 4, 0:NT * NE]))
                for t in range(NT):
                    top = part(F, 2560 + 64 * t, 8)
                    idx = part(F, 2568 + 64 * t, 8).bitcast(U32)
                    idf = part(F, 2576 + 64 * t, 8)
                    one = part(F, 2584 + 64 * t, 2, 8)
                    mine = lg[:, t * NE:(t + 1) * NE]
                    link(v.max(top, mine))
                    link(v.max_index(idx, top, mine))
                    link(v.tensor_copy(idf, idx))
                    for r in range(2):
                        link(v.tensor_scalar(one[:, r, :], iota[:, 0:NE], idf[:, r:r + 1], None, ALU.is_equal))
                    link(v.tensor_tensor(st[:, 8 + t:9 + t], top[:, 1:2], top[:, 0:1], ALU.subtract))
                    last = v.tensor_tensor(rs[:, t * NE:(t + 1) * NE], one[:, 0, :], one[:, 1, :], ALU.add)
                    link(last)
                v.tensor_copy(mark[:, 10:11], cact[:, 0:1]).then_inc(sem("chosen"), 1)
                v.tensor_copy(mark[:, 11:12], cact[:, 0:1]).then_inc(sem("w_dif"), 1)
                dve.wait_ge(sem("hnat_ps"), 1)
                v.tensor_copy(hnat[:, 1, :], bank2(2)).then_inc(sem("hnat"), 1)
                dve.wait_ge(sem("w_exp"), 1)
                link(v.tensor_scalar(st[:, 10:12], st[:, 8:10], 1.0, None, ALU.add))
                link(v.reciprocal(st[:, 10:12], st[:, 10:12]))
                link(v.tensor_tensor(st[:, 8:10], st[:, 8:10], st[:, 10:12], ALU.mult))
                for t in range(NT):
                    one = part(F, 2584 + 64 * t, 2, 8)
                    link(v.tensor_scalar(one[:, 1, :], one[:, 1, :], st[:, 8 + t:9 + t], None, ALU.mult))
                    link(v.scalar_tensor_tensor(out=wts[:, t, :], in0=one[:, 0, :], scalar=st[:, 10 + t:11 + t],
                                                in1=one[:, 1, :], op0=ALU.mult, op1=ALU.add))
                dve.wait_ge(sem("rank_ps"), 1)
                pm = posm.rearrange("p t e -> p (t e)")
                link(v.scalar_tensor_tensor(out=pm, in0=ps[:, 5, 0:NT * NE], scalar=1.0, in1=rs[:, 0:NT * NE],
                                            op0=ALU.add, op1=ALU.mult))
                link(v.tensor_scalar(pm, pm, -1.0, None, ALU.add))
                nb = part(F, 2700, NE)
                tmp = part(F, 2708, NE)
                inc = part(F, 2716, NE)
                cnt = part(F, 2724, NE)
                link(v.tensor_copy(cnt, ps[:, 6, 0:NE]))
                link(v.tensor_scalar(nb, cnt, float(BLK), 1.0, ALU.is_gt, ALU.add))
                for k in range(2, NBLK):
                    link(v.tensor_scalar(tmp, cnt, float(k * BLK), None, ALU.is_gt))
                    link(v.tensor_tensor(nb, nb, tmp, ALU.add))
                link(v.tensor_scalar(tmp, nb, 0.0, 1.0, ALU.mult, ALU.add))
                link(v.tensor_tensor_scan(inc, tmp, nb, 0.0, ALU.mult, ALU.add))
                link(v.tensor_tensor(inc, inc, nb, ALU.subtract))
                v.tensor_copy(meta[:, 0:NE], nb)
                link(v.tensor_copy(meta[:, NE:2 * NE], inc))
                v.tensor_copy(mark[:, 12:13], cact[:, 0:1]).then_inc(sem("meta"), 1)
                gate = adav[:, 3, 16:24].unsqueeze(2).broadcast_to([P, KD, BLK])
                with dve.Fori(0, NE) as e:
                    n = dve.value_load(meta[0:1, bass.ds(e, 1)], min_val=1, max_val=NBLK)
                    cum = dve.value_load(meta[0:1, bass.ds(e + NE, 1)], min_val=0, max_val=NBLK * NE)
                    with dve.Fori(0, n) as b:
                        dve.wait_ge(sem("gath_ps"), cum + b)
                        dve.wait_ge(sem("spread_ps"), cum)
                        for t in range(NT):
                            last = v.tensor_scalar(sel[:, t, :], iota[:, bass.ds(b * BLK, BLK)],
                                                   posm[:, t, bass.ds(e, 1)], None, ALU.is_equal)
                        last.then_inc(sem("sel"), 1)
                    with dve.Fori(0, EH) as half:
                        q0 = e * ECHUNKS + half * SLOTS
                        for s in range(SLOTS):
                            with dve.Fori(0, n) as b:
                                dve.wait_ge(sem("e_tanh"), q0 + s + 1)
                                v.scalar_tensor_tensor(out=e_tg[:, bass.ds(b, 1), :], in0=e_tg[:, bass.ds(b, 1), :],
                                                       scalar=1.0, in1=ps[:, bass.ds(b, 1), 0:FT * BLK], op0=ALU.add,
                                                       op1=ALU.mult)
                            v.tensor_copy(mark[:, 13:14], cact[:, 0:1]).then_inc(sem("e_mid"), 1)
                            with dve.Fori(0, n) as b:
                                dve.wait_ge(sem("e_mid"), q0 + s + 1)
                                v.scalar_tensor_tensor(out=e_hid[:, s % 2, bass.ds(b, 1), :],
                                                       in0=e_tg[:, bass.ds(b, 1), :], scalar=0.5,
                                                       in1=ps[:, bass.ds(b, 1), FT * BLK:2 * FT * BLK], op0=ALU.mult,
                                                       op1=ALU.mult)
                            v.tensor_copy(mark[:, 14:15], cact[:, 0:1]).then_inc(sem("e_hid"), 1)
                    with dve.Fori(0, n) as b:
                        dve.wait_ge(sem("e_used"), e * ECHUNKS + ECHUNKS)
                        done = cum + b
                        dve.wait_ge(sem("y_ps"), done)
                        for t in range(NT):
                            last = v.tensor_scalar(sel[:, t, :], iota[:, bass.ds(b * BLK, BLK)],
                                                   posm[:, t, bass.ds(e, 1)], wts[:, t, bass.ds(e, 1)],
                                                   ALU.is_equal, ALU.mult)
                        last.then_inc(sem("sw"), 1)
                        v.tensor_tensor(yT, ps[:, bass.ds(b + 4, 1), :].rearrange("p b (k n) -> p (b k) n", k=KD),
                                        gate, ALU.mult).then_inc(sem("yT"), 1)
                        dve.wait_ge(sem("spread_ps"), done + 1)
                        for i, bank in enumerate((3, 0, 1, 2)):
                            t, half = i // 2, i % 2
                            xs = x[:, t, half * 512:(half + 1) * 512]
                            last = v.tensor_tensor(xs, xs, ps[:, bank, :], ALU.add)
                        last.then_inc(sem("x_add"), 1)
                        dve.wait_ge(sem("x_add"), done + 1)
                v.tensor_copy(mark[:, 15:16], cact[:, 0:1]).then_inc(sem("x_final"), 1)

            for l in range(DEPTH):
                mixer(l)
                if l == 0:
                    dense()
                else:
                    experts()


_INS = ["x", "c", "positions", "w_ada", "b_ada", "norm_gain", "w_in", "latent_gain", "w_q_up", "w_kv_up", "q_gain",
        "k_gain", "conv_w", "conv_b", "w_a", "b_a", "w_x", "b_x", "lru_lambda", "out_gain", "w_out", "ffn_w_gate",
        "ffn_w_up", "ffn_w_down", "router_w", "moe_w_gate", "moe_w_up", "moe_w_down"]


def kernel(**inputs):
    import concourse.bacc as bacc
    from concourse.bass_utils import run_bass_kernel_spmd

    nc = bacc.Bacc("TRN2", target_bir_lowering=False, num_devices=1)
    arrays, args = {}, []
    for name in _INS:
        a = np.ascontiguousarray(inputs[name])
        arrays[f"in_{name}"] = a
        args.append(nc.dram_tensor(f"in_{name}", a.shape, mybir.dt.from_np(a.dtype), kind="ExternalInput").ap())
    shape = arrays["in_x"].shape
    args.append(nc.dram_tensor("out_x", shape, F32, kind="ExternalOutput").ap())
    trunk(nc, *args)
    r = run_bass_kernel_spmd(nc, [arrays], core_ids=[0])
    return r.results[0]["out_x"]
```

```python
from contextlib import ExitStack

import numpy as np

import concourse.bass as bass
from concourse import mybir
from concourse.alu_op_type import AluOpType as ALU

F32 = mybir.dt.float32
F32R = mybir.dt.float32r
I32 = mybir.dt.int32
U32 = mybir.dt.uint32
ACT = mybir.ActivationFunctionType
AX = mybir.AxisListType.X

P = 128
EPS = 1e-6
NEG = -1e30
GELU_A = 0.044715
GELU_B = float(np.sqrt(2.0 / np.pi))
FT = 2
EFT = 4
SLOTS = 7
SPLITS = 3
TWO_PI = 2.0 * np.pi


def cody_waite():
    c1 = 6.28125
    c2 = float(np.round((TWO_PI - c1) * 2.0 ** 21) / 2.0 ** 21)
    return c1, c2, float(np.float32(TWO_PI - c1 - c2))


def trunk(nc, x_in, c_in, pos_in, w_ada, b_ada, norm_gain, w_in, latent_gain, w_q_up, w_kv_up, q_gain, k_gain,
          conv_w, conv_b, w_a, b_a, w_x, b_x, lru_lambda, out_gain, w_out, ffn_gate, ffn_up, ffn_down,
          router_w, moe_gate, moe_up, moe_down, out):
    _, SEQ, D = x_in.shape
    DEPTH = w_ada.shape[0]
    IN_COLS = w_in.shape[2]
    Q_RANK = w_q_up.shape[1]
    KV_RANK = w_kv_up.shape[1]
    LRU = conv_w.shape[2]
    TAPS = conv_w.shape[1]
    QK = q_gain.shape[1]
    NOPE = 64
    ROPE = QK - NOPE
    HALF = ROPE // 2
    H = w_q_up.shape[2] // QK
    V = w_kv_up.shape[2] // H - NOPE
    D_FF = ffn_gate.shape[2]
    NE = router_w.shape[2]
    D_FFE = moe_gate.shape[3]
    LAT = Q_RANK + KV_RANK + ROPE
    NT = SEQ // P
    KD = D // P
    LT = LRU // P
    FW = FT * P
    CHUNKS = D_FF // FW
    EW = EFT * P
    ECHUNKS = D_FFE // EW
    SCALE = float(QK) ** -0.5
    assert NT == 2 and KD == 8 and LT == 4 and H == 8 and V == 64 and D_FF % FW == 0 and D_FFE % EW == 0
    assert DEPTH == 2 and Q_RANK == 256 and KV_RANK == 128
    inv_freq = [float(np.float32(1e4) ** np.float32(-2 * i / ROPE)) for i in range(HALF)]

    with ExitStack() as ctx:
        def sb(name, cols, dt=F32):
            return ctx.enter_context(nc.sbuf_tensor(name, [P, cols], dt))

        def two_views(name, cols):
            with nc.sbuf_tensor(f"{name}_r", [P, cols], F32R) as rounded:
                pass
            return sb(name, cols), rounded

        sems = {}

        def sem(name):
            if name not in sems:
                sems[name] = ctx.enter_context(nc.semaphore(name))
            return sems[name]

        ps = ctx.enter_context(nc.psum_tensor("ps", [P, 8, 512], F32))
        PIECE = KD * EW
        HALFP = PIECE // 2
        arena = sb("arena", SLOTS * PIECE)
        CELL = 3 * D
        CELLS = SLOTS * PIECE // CELL
        WORK0 = 3
        work = arena[:, WORK0 * CELL:CELLS * CELL]
        x = sb("x", NT * D)[:, :].rearrange("p (t d) -> p t d", t=NT)
        hT, hTr = (v[:, :].rearrange("p (k n) -> p k n", k=KD) for v in two_views("hT", KD * SEQ))
        F, Fr = two_views("F", 3724)
        ident = sb("ident", P)
        ones = sb("ones", P)
        zero = sb("zero", 2)
        iota = sb("iota", SEQ)
        colA = sb("colA", 126)
        colB = sb("colB", 96)
        adav = sb("adav", 4 * 24)[:, :].rearrange("p (a n) -> p a n", a=4)
        adaA = sb("adaA", 4 * KD)[:, :].rearrange("p (a n) -> p a n", a=4)
        cact = sb("cact", KD)
        hb = sb("hb", 16)
        m2ls = sb("m2ls", 2 * LT)
        st = sb("st", 48)
        rs = sb("rs", 48)
        mx = sb("mx", 2 * H)
        den = sb("den", 2 * H)
        mark = sb("mark", 16)
        posm = sb("posm", NT * NE)[:, :].rearrange("p (t e) -> p t e", t=NT)
        wts = sb("wts", NT * NE)[:, :].rearrange("p (t e) -> p t e", t=NT)
        meta = sb("meta", 2 * (2 * NE + 1) + 1, I32)
        split, splitr = two_views("split", 2 * SPLITS * HALFP)
        wh = splitr[:, 0:SPLITS * HALFP].rearrange("p (s n) -> p s n", s=SPLITS)
        wl = splitr[:, SPLITS * HALFP:].rearrange("p (s n) -> p s n", s=SPLITS)
        tokens, tokensr = two_views("tokens", 3 * D)

        def part(buf, at, *dims):
            n = int(np.prod(dims))
            v = buf[:, at:at + n]
            if len(dims) == 1:
                return v
            names = "abcd"[:len(dims)]
            return v.rearrange(f"p ({' '.join(names)}) -> p {' '.join(names)}",
                               **{k: d for k, d in zip(names[1:], dims[1:])})

        xn = part(F, 0, NT, D)
        gr = part(F, 0, LT, SEQ)
        cT = part(F, 1024, 3, SEQ)
        xp = part(F, 1792, LT, SEQ + TAPS - 1)
        mask = part(F, 2828, SEQ)
        gains = part(F, 3084, 4, QK)
        cs = part(F, 3468, NT, 2, HALF)
        rw = part(F, 3532, KD, NE)
        tri = part(F, 3596, P)
        lq = part(arena, CELLS * CELL, LT, SEQ)
        wq = part(work, 0, 2, H * QK)
        wkv = part(work, 1536, H * (NOPE + V))
        wbd = part(work, 2560, 2, LT, P)
        kT = part(work, 3584, H, SEQ)
        mT = part(work, 3584, KD, SEQ)
        qn = part(work, 5632, NT, H, QK)
        kn = part(work, 7168, NT, H, QK)
        PT = part(work, 5632, NT + 1, H, P)
        v_sb = part(work, 8704, NT, H * V)
        s1 = part(work, 9728, H, SEQ)
        s0 = part(work, 11776, H, P)
        osb = part(work, 9728, NT, H, V)
        rbc = part(work, 9728 + NT * H * V, SEQ)
        sq = part(work, 12800, 832)
        cn = part(work, 12800, NT, LAT)
        lx = part(work, 13632, LT, SEQ)
        la = part(work, 14656, LT, SEQ)
        li = part(work, 15680, LT, SEQ)
        lr = part(work, 16704, LT, SEQ)
        rope_tmp = part(work, 17728, 4, H, HALF)
        qT = hT
        ygT = hT
        rowsA = part(work, 0, P)
        rowsB = part(work, P, P)
        f_tg = part(F, 0, FT * SEQ)
        f_hid = part(F, FT * SEQ, FT * SEQ)
        hh = part(tokensr, 0, KD, SEQ)
        hl = hTr
        fh = part(tokensr, KD * SEQ, 2, FT * SEQ)
        fl = part(Fr, 2 * FT * SEQ, 2, FT * SEQ)
        hTh = part(tokensr, 0, KD, P)
        hTl = part(tokensr, KD * P, KD, P)
        fTs = part(tokensr, 2 * KD * P, 2, EFT * P)
        hnat = part(F, 0, NT, D)
        e_tg = part(F, 2048, EW)
        e_hid = part(F, 2560, EW)
        fTs_last = part(Fr, 2048, 2, EFT * P)
        sel = part(F, 3072, NT, P)
        swT = part(F, 3328, NT * P)
        ynat = hT[:, 0:KD // 2, :].rearrange("p k n -> p (k n)")
        gate_cols = part(tokens, 0, KD, P)
        gate_row = hT[:, KD // 2:KD, :].rearrange("p k n -> p (k n)")
        pos_i = sb("pos_i", NT, I32)
        pos_f = sb("pos_f", NT)
        ivf = part(work, 2 * P, HALF)
        ang = part(work, 3 * P, 2, NT, HALF)
        angk = part(work, 4 * P, 2, NT, HALF)

        C0, NG, OG, LG, CW, CB, BA, BX, LM = 0, 8, 40, 56, 62, 94, 102, 110, 118

        SPLIT0, TOKENS = CELLS, CELLS + 2 * SPLITS * HALFP // CELL

        def place(cell, cols):
            if cell < CELLS:
                return arena[:, cell * CELL:cell * CELL + cols]
            if cell < TOKENS:
                return split[:, (cell - SPLIT0) * CELL:(cell - SPLIT0) * CELL + cols]
            return tokens[:, 0:cols]

        units = [("g", 0), ("u", 0)]
        for c in range(1, CHUNKS):
            units += [("g", c), ("u", c), ("d", c - 1)]
        units.append(("d", CHUNKS - 1))
        fills = [("ada", 0, k, c, []) for k, c in enumerate((0, 1, 2, 4, 5, 6, 7, 8))]
        fills += [("win", 0, i, SPLIT0 + i, []) for i in range(4)]
        fills += [("small", 0, 0, None, [("wbd_zero", 1)])]
        fills += [("ada", 1, k, c, w) for k, (c, w) in enumerate((
            (TOKENS, []), (0, [("ada_step0", 2)]), (1, [("ada_step0", 3)]), (2, [("ada_step0", 4)]),
            (0, [("ada_step1", 3)]), (1, [("ada_step1", 4)]), (2, [("ada_step1", 5)]), (0, [("ada_step1", 6)])))]
        fills += [("wout", 0, i, SPLIT0 + i, [("z_done", 1)]) for i in range(3)]
        fills += [("ada", 2, k, c, w) for k, (c, w) in enumerate((
            (1, [("ada_step1", 7)]), (2, [("ada_step1", 8)]), (12, []), (1, [("ada_step1", 10)]),
            (2, [("ada_step1", 11)]), (12, [("ada_step1", 12)]), (1, [("ada_step1", 13)]), (2, [("ada_step1", 14)])))]
        ada3 = [("ada", 3, k, (1, 0)[k % 2], [("ada_step1", 16) if k == 0 else ("ada_red", 2) if k == 1 else
                                              ("ada_step1", 16 + k)]) for k in range(KD)]
        ffn = [("ffn", 0, c, WORK0 + 2 * (c % 3),
                [("f_lo", units.index(("d", c - 3)) + 1) if c >= 3 else ("wout_done", 1)]) for c in range(CHUNKS)]
        fills += ffn[:3]
        for c in range(3, CHUNKS):
            fills += [ffn[c], ada3[c - 3]]
        assert CHUNKS - 3 == KD
        fills += [
            ("win", 1, 0, 1, [("ada_step1", 24)]),
            ("win", 1, 1, 6, [("f_lo", 3 * CHUNKS)]),
            ("win", 1, 2, 2, [("ada_red", 3)]),
            ("win", 1, 3, 0, [("ada_red", 4)]),
            ("small", 1, 0, None, [("wbd_zero", 2)]),
            ("wout", 1, 0, 9, [("f_wused", 3 * CHUNKS)]),
            ("wout", 1, 1, 10, []),
            ("wout", 1, 2, 11, []),
        ]
        pieces = [("g", 0), ("u", 0)]
        for c in range(1, ECHUNKS):
            pieces += [("g", c), ("u", c), ("d", c - 1)]
        pieces.append(("d", ECHUNKS - 1))
        NP = len(pieces)
        HP = 2 * NP
        assert NP % SLOTS == 0 and HP % SPLITS == 0
        for i in range(SLOTS):
            fills.append(("moe", 0, i, None, {0: [("z_done", 2)], 2: [("rg_ps", 2)], 3: [("wout_done", 2)]}.get(i, [])))
        n_dma = {"ada": 1, "win": 1, "wout": 1, "small": 6}
        landed, total = {}, {}
        for kind, a, i, cell, _ in fills:
            if kind in n_dma:
                total[cell] = total.get(cell, 0) + 16 * n_dma[kind]
                landed[kind, a, i] = (cell, total[cell])

        def fill_sem(cell):
            return sem("small_in" if cell is None else f"place{cell}_in")

        def wait_fill(eng, kind, a, i):
            cell, value = landed[kind, a, i]
            eng.wait_ge(fill_sem(cell), value)
            return cell

        def unit(kind, c):
            at = (WORK0 + 2 * (c % 3)) * CELL + "gud".index(kind) * HALFP
            return arena[:, at:at + HALFP]

        TABLE = 2 * NE + 1
        COUNT = 2 * TABLE

        def fT_parts(c):
            both = fTs_last if c == ECHUNKS - 1 else fTs
            return both[:, 0, :], both[:, 1, :]

        def piece_slot(i):
            return i % SLOTS

        def piece_half(j):
            j = j % HP
            at = piece_slot(j // 2) * PIECE + (j % 2) * HALFP
            return arena[:, at:at + HALFP]

        def bank2(b, n=2):
            return ps[:, b:b + n, :].rearrange("p b n -> p (b n)")

        up_done = {c: 2 * pieces.index(("u", c)) + 1 for c in range(ECHUNKS)}
        turn_after = {up_done[c] + (2 if c < ECHUNKS - 1 else 1): c for c in range(ECHUNKS)}
        GATHER_AFTER = up_done[ECHUNKS - 1]
        SWT_AFTER = SPLIT_H_AFTER = GATHER_AFTER + 2
        assert (ECHUNKS - 1) % 2 == 0
        silu_after = {j: c for c, j in up_done.items()}

        block = ctx.enter_context(nc.Block())

        @block.sync
        def _(sp):
            sp.dma_start(x[:, :, :], x_in[0].rearrange("(t p) d -> p t d", p=P)).then_inc(sem("x_in"), 16)

            def piece(i, e):
                kind, c = pieces[i]
                at = piece_slot(i) * PIECE
                es = bass.ds(e, 1)
                if kind == "d":
                    src = moe_down[0, es, c * EW:(c + 1) * EW, :].rearrange("e (f p) n -> p (e f) n", p=P)
                    dst = part(arena, at, EFT, D)
                else:
                    w = moe_gate if kind == "g" else moe_up
                    src = w[0, es, :, c * EW:(c + 1) * EW].rearrange("e (k p) f -> p (e k) f", p=P)
                    dst = part(arena, at, KD, EW)
                sp.dma_start(dst, src).then_inc(sem(f"piece{piece_slot(i)}_in"), 16)

            for n, (kind, a, i, cell, waits) in enumerate(fills):
                if n == 1:
                    sp.wait_ge(sem("rowsA_in"), 16 * 9)
                for name, value in waits:
                    sp.wait_ge(sem(name), value)
                if kind == "moe":
                    piece(i, 0)
                    continue
                if kind == "ffn":
                    f = slice(i * FW, (i + 1) * FW)
                    for u, src, dims in (("g", ffn_gate[0][:, f].rearrange("(k p) f -> p k f", p=P), (KD, FW)),
                                         ("u", ffn_up[0][:, f].rearrange("(k p) f -> p k f", p=P), (KD, FW)),
                                         ("d", ffn_down[0][f, :].rearrange("(f p) n -> p f n", p=P), (FT, D))):
                        sp.dma_start(part(unit(u, i), 0, *dims), src).then_inc(sem(f"ffn_{u}{i % 3}_in"), 16)
                    continue
                s = fill_sem(cell)
                if kind == "ada":
                    sp.dma_start(place(cell, 3 * D), w_ada[a // 2, a % 2, i * P:(i + 1) * P, :]).then_inc(s, 16)
                elif kind == "win":
                    sp.dma_start(part(place(cell, 2 * IN_COLS), 0, 2, IN_COLS),
                                 w_in[a, i * 2 * P:(i + 1) * 2 * P, :].rearrange("(k p) n -> p k n", p=P))\
                        .then_inc(s, 16)
                elif kind == "wout":
                    n = min(3, KD - 3 * i)
                    sp.dma_start(part(place(cell, n * D), 0, n, D),
                                 w_out[a, i * 3 * P:(i * 3 + n) * P, :].rearrange("(k p) n -> p k n", p=P))\
                        .then_inc(s, 16)
                else:
                    sp.dma_start(wq, w_q_up[a].rearrange("(k p) n -> p k n", p=P)).then_inc(s, 16)
                    sp.dma_start(wkv, w_kv_up[a]).then_inc(s, 16)
                    for g, w in enumerate((w_a, w_x)):
                        pair = w[a].rearrange("(i two) r c -> two r i c", two=2)
                        for two in range(2):
                            r = slice(64 * two, 64 * two + 64)
                            sp.dma_start(wbd[r, g, :, r], pair[two]).then_inc(s, 16)

            def rest(p, e, n0, n1):
                for i in range(n0, n1):
                    n = i + (pieces[min(i + 1, NP - 1)] == ("d", 0))
                    if pieces[i] != ("d", 0):
                        sp.wait_ge(sem("w_lo"), p * HP + 2 * (n - SLOTS) + 2)
                    piece(i, e)
            rest(0, 0, SLOTS, NP)
            sp.wait_ge(sem("meta"), 1)
            passes = sp.value_load(meta[0:1, COUNT:COUNT + 1], min_val=NE, max_val=2 * NE)
            AHEAD = (SPLITS + 1) // 2
            rest(1, sp.value_load(meta[0:1, 1:2], min_val=0, max_val=NE - 1), 0, AHEAD)
            with sp.Fori(1, passes) as p:
                e, e_next = (sp.value_load(meta[0:1, bass.ds(q, 1)], min_val=0, max_val=NE - 1) for q in (p, p + 1))
                rest(p, e, AHEAD, NP)
                rest(p + 1, e_next, 0, AHEAD)

            sp.wait_ge(sem("x_final"), 1)
            sp.dma_start(out[0].rearrange("(t p) d -> p t d", p=P), x[:, :, :]).then_inc(sem("out"), 16)
            sp.wait_ge(sem("out"), 16)

        @block.gpsimd
        def _(pool):
            g = nc.gpsimd
            g.memset(ident[:, :], 0.0).then_inc(sem("g0"), 1)
            g.memset(ones[:, :], 1.0).then_inc(sem("g0"), 1)
            g.memset(zero[:, :], 0.0).then_inc(sem("g0"), 1)
            g.memset(tri, 1.0).then_inc(sem("g0"), 1)
            g.memset(mask, 0.0).then_inc(sem("g0"), 1)
            for i, f in enumerate(inv_freq):
                g.memset(ivf[:, i:i + 1], f).then_inc(sem("g0"), 1)
            pool.wait_ge(sem("g0"), 5 + HALF)
            g.affine_select(out=ident[:, :], in_=ident[:, :], compare_op=ALU.not_equal, fill=1.0, base=0,
                            pattern=[[-1, P]], channel_multiplier=1).then_inc(sem("consts"), 1)
            g.affine_select(out=tri, in_=tri, compare_op=ALU.is_gt, fill=0.0, base=0,
                            pattern=[[1, P]], channel_multiplier=-1).then_inc(sem("consts"), 1)
            g.affine_select(out=mask[:, P:2 * P], in_=mask[:, P:2 * P], compare_op=ALU.is_ge, fill=NEG, base=0,
                            pattern=[[-1, P]], channel_multiplier=1).then_inc(sem("consts"), 1)
            g.iota(iota[:, :], pattern=[[1, SEQ]], base=0, channel_multiplier=0,
                   allow_small_or_imprecise_dtypes=True).then_inc(sem("consts"), 1)

            def ada(a):
                for k in range(KD):
                    w = place(wait_fill(pool, "ada", a, k), 3 * D)
                    n = (a - 1) * KD + k
                    if k == 0:
                        g.tensor_scalar(w, w, cact[:, 0:1], 0.0, ALU.mult, ALU.add).then_inc(sem("ada_step1"), 1)
                    else:
                        g.tensor_scalar(w, w, cact[:, k:k + 1], 0.0, ALU.mult, ALU.add).then_inc(sem("g_prod"), 1)
                        pool.wait_ge(sem("g_prod"), n - a + 1)
                        g.tensor_tensor(w, w, prev, ALU.add).then_inc(sem("ada_step1"), 1)
                    pool.wait_ge(sem("ada_step1"), n + 1)
                    prev = w

            for l in range(DEPTH):
                if l:
                    pool.wait_ge(sem("f_lo"), 3 * CHUNKS)
                    pool.wait_ge(sem("xT_ps"), 3)
                else:
                    pool.wait_ge(sem("cols_in"), 1)
                    pool.wait_ge(sem("xT_ps"), 1)
                    pool.wait_ge(sem("setup"), 2)
                    pool.wait_ge(sem("ada_step0"), 5)
                g.memset(wbd[:, 0, :, :], 0.0).then_inc(sem("g2"), 1)
                g.memset(wbd[:, 1, :, :], 0.0).then_inc(sem("g2"), 1)
                g.memset(xp[:, :, 0:TAPS - 1], 0.0).then_inc(sem("pad"), 1)
                pool.wait_ge(sem("g2"), 2 * (l + 1))
                pool.wait_ge(sem("pad"), l + 1)
                g.memset(mark[:, 0:1], 0.0).then_inc(sem("wbd_zero"), 1)
                if l == 0:
                    for a in (1, 2, 3):
                        ada(a)
            pool.wait_ge(sem("hnat_ps"), 1)
            g.memset(swT, 0.0).then_inc(sem("no_outputs"), 1)
            g.memset(ynat, 0.0).then_inc(sem("no_outputs"), 1)
            pool.wait_ge(sem("no_outputs"), 2)
            g.memset(mark[:, 3:4], 0.0).then_inc(sem("y_sb"), 1)

        @block.tensor
        def _(pe):
            mm = nc.tensor.matmul
            tr = nc.tensor.transpose

            def ada_reduce(a):
                if a == 0:
                    pe.wait_ge(sem("ada_step0"), KD)
                else:
                    pe.wait_ge(sem("ada_step1"), KD * a)
                acc = place(landed["ada", a, KD - 1][0], 3 * D)
                for j in range(3 * KD):
                    last = mm(ps[:, 4 + (a == 3), j:j + 96], acc[:, j * P:(j + 1) * P], ones[:, 0:96],
                              start=True, stop=True)
                last.then_inc(sem("ada_red"), 1)

            def norm_transposes(n):
                pe.wait_ge(sem("xn"), n + 1)
                for j in range(KD):
                    for t in range(NT):
                        last = tr(ps[:, j // 2, (j % 2) * SEQ + t * P:(j % 2) * SEQ + (t + 1) * P],
                                  xn[:, t, j * P:(j + 1) * P], ident[:, :])
                last.then_inc(sem("xT_ps"), 1)

            def h_ready(n):
                pe.wait_ge(sem("hT_act"), n + 1)
                pe.wait_ge(sem("hT_dve"), n + 1)

            def residual_transposes(n):
                pe.wait_ge(sem("yg"), n + 1)
                for t in range(NT):
                    for j in range(KD):
                        last = tr(ps[:, 2 * t + j // 4, (j % 4) * P:(j % 4 + 1) * P], ygT[:, j, t * P:(t + 1) * P],
                                  ident[:, :])
                last.then_inc(sem("res_ps"), 1)

            def mixer(l):
                norm_transposes(2 * l)
                if l == 0:
                    ada_reduce(0)
                h_ready(2 * l)
                parts = [part(place(wait_fill(pe, "win", l, i), 2 * IN_COLS), 0, 2, IN_COLS) for i in range(4)]

                def win(k, a, b):
                    return parts[k // 2][:, k % 2, a:b]

                for t in range(NT):
                    for k in range(KD):
                        last = mm(ps[:, 4 + t, 0:LAT], hT[:, k, t * P:(t + 1) * P], win(k, 0, LAT),
                                  start=(k == 0), stop=(k == KD - 1))
                    last.then_inc(sem("lat_ps"), 1)
                for part_, b0 in ((0, 6), (1, 0)):
                    for i in range(LT):
                        c0 = LAT + part_ * LRU + i * P
                        for k in range(KD):
                            last = mm(ps[:, b0 + i // 2, (i % 2) * SEQ:(i % 2 + 1) * SEQ], win(k, c0, c0 + P),
                                      hT[:, k, :], start=(k == 0), stop=(k == KD - 1))
                    last.then_inc(sem("rec_ps"), 1)
                last = mm(ps[:, 3, 0:1], ident[:, :], zero[:, 0:1], start=True, stop=True)
                last.then_inc(sem("z_done"), 1)
                pe.wait_ge(sem("cn"), l + 1)
                for i in range(3):
                    for t in range(NT):
                        last = tr(ps[:, 2 + i // 2, (i % 2) * SEQ + t * P:(i % 2) * SEQ + (t + 1) * P],
                                  cn[:, t, i * P:(i + 1) * P], ident[:, :])
                last.then_inc(sem("cT_ps"), 1)
                pe.wait_ge(sem("cT"), l + 1)
                wait_fill(pe, "small", l, 0)
                for t, (bq, bk) in enumerate(((4, 2), (6, 0))):
                    if t == 1:
                        pe.wait_ge(sem("rec_sb"), l + 1)
                    for half in range(2):
                        w = H * QK // 2
                        for k in range(2):
                            mm(ps[:, bq + half, 0:w], cT[:, k, t * P:(t + 1) * P], wq[:, k, half * w:(half + 1) * w],
                               start=(k == 0), stop=(k == 1))
                    for half in range(2):
                        last = mm(ps[:, bk + half, :], cT[:, 2, t * P:(t + 1) * P], wkv[:, half * 512:(half + 1) * 512],
                                  start=True, stop=True)
                    last.then_inc(sem("up_ps"), 1)
                for t, (bq, bk) in enumerate(((4, 2), (6, 0))):
                    pe.wait_ge(sem("qk"), 2 * l + t + 1)
                    pe.wait_ge(sem("v"), 2 * l + t + 1)
                    for src, b0 in ((qn, bq), (kn, bk)):
                        for h in range(H):
                            last = tr(ps[0:QK, b0 + h // 4, (h % 4) * P:(h % 4 + 1) * P], src[:, t, h, :], ident[:, :])
                    last.then_inc(sem("qkT_ps"), 1)
                pe.wait_ge(sem("qT"), 2 * l + 2)
                pe.wait_ge(sem("kT"), 2 * l + 2)
                for h in range(H):
                    last = mm(ps[:, 2 + h // 2, (h % 2) * SEQ:(h % 2 + 1) * SEQ], qT[0:QK, h, P:2 * P], kT[0:QK, h, :],
                              start=True, stop=True)
                last.then_inc(sem("s_ps"), 1)
                pe.wait_ge(sem("xr"), l + 1)
                for g, b0 in ((0, 6), (1, 0)):
                    for i in range(LT):
                        last = mm(ps[:, b0 + i // 2, (i % 2) * SEQ:(i % 2 + 1) * SEQ], wbd[:, g, i, :], lx[:, i, :],
                                  start=True, stop=True)
                last.then_inc(sem("rg_ps"), 1)
                pe.wait_ge(sem("rg"), l + 1)
                for h in range(H):
                    last = mm(ps[:, h // 4, (h % 4) * P:(h % 4 + 1) * P], qT[0:QK, h, 0:P], kT[0:QK, h, 0:P],
                              start=True, stop=True)
                last.then_inc(sem("s_ps"), 1)
                pe.wait_ge(sem("p"), 2 * l + 1)
                for kt in range(NT):
                    for h in range(H):
                        last = tr(ps[:, 2 + 2 * kt + h // 4, (h % 4) * P:(h % 4 + 1) * P],
                                  s1[:, h, kt * P:(kt + 1) * P], ident[:, :])
                last.then_inc(sem("pT_ps"), 1)
                pe.wait_ge(sem("p"), 2 * l + 2)
                for h in range(H):
                    last = tr(ps[:, h // 4, (h % 4) * P:(h % 4 + 1) * P], s0[:, h, :], ident[:, :])
                last.then_inc(sem("pT_ps"), 1)
                pe.wait_ge(sem("pT_a"), 2 * l + 1)
                pe.wait_ge(sem("pT_d"), l + 1)
                for h in range(H):
                    for kt in range(NT):
                        last = mm(ps[:, 7, h * V:(h + 1) * V], PT[:, 1 + kt, h, :], v_sb[:, kt, h * V:(h + 1) * V],
                                  start=(kt == 0), stop=(kt == NT - 1))
                last.then_inc(sem("o_ps"), 1)
                pe.wait_ge(sem("pT_a"), 2 * l + 2)
                for h in range(H):
                    last = mm(ps[:, 6, h * V:(h + 1) * V], PT[:, 0, h, :], v_sb[:, 0, h * V:(h + 1) * V],
                              start=True, stop=True)
                last.then_inc(sem("o_ps"), 1)
                pe.wait_ge(sem("recsq"), l + 1)
                for i in range(LT):
                    last = mm(ps[:, 2, 0:SEQ], ones[:, :], la[:, i, :], start=(i == 0), stop=(i == LT - 1))
                last.then_inc(sem("rss_ps"), 1)
                pe.wait_ge(sem("on"), l + 1)
                for i in range(LT):
                    for t in range(NT):
                        last = tr(ps[:, i // 2, (i % 2) * SEQ + t * P:(i % 2) * SEQ + (t + 1) * P],
                                  osb[:, t, 2 * i:2 * i + 2, :].rearrange("p a b -> p (a b)"), ident[:, :])
                last.then_inc(sem("onT_ps"), 1)
                pe.wait_ge(sem("mT"), l + 1)
                parts = [part(place(wait_fill(pe, "wout", l, i), 3 * D), 0, 3, D) for i in range(3)]
                for j in range(KD):
                    for k in range(KD):
                        last = mm(ps[:, 4 + j // 2, (j % 2) * SEQ:(j % 2 + 1) * SEQ],
                                  parts[k // 3][:, k % 3, j * P:(j + 1) * P], mT[:, k, :],
                                  start=(k == 0), stop=(k == KD - 1))
                last.then_inc(sem("wout_done"), 1)
                residual_transposes(2 * l)
                if l == 0:
                    pe.wait_ge(sem("yg"), 1)
                    ada_reduce(1)

            def dense():
                norm_transposes(1)

                def triple(out_, w, xh, xl, first, last_):
                    h, lo = (s[:, w[0], w[1]:w[1] + P] for s in (wh, wl))
                    mm(out_, h, xh, start=first, stop=False, skip_group_check=True)
                    mm(out_, h, xl, start=False, stop=False, skip_group_check=True)
                    return mm(out_, lo, xh, start=False, stop=last_, skip_group_check=True)

                for n, (kind, c) in enumerate(units):
                    pe.wait_ge(sem("f_lo"), n + 1)
                    if kind == "d":
                        pe.wait_ge(sem("fl"), c + 1)
                        for f in range(FT):
                            fs = slice(f * SEQ, (f + 1) * SEQ)
                            for j in range(KD):
                                last = triple(ps[:, 4 + j // 2, (j % 2) * SEQ:(j % 2 + 1) * SEQ],
                                              (n % SPLITS, f * D + j * P), fh[:, c % 2, fs], fl[:, c % 2, fs],
                                              c == 0 and f == 0 and j % 2 == 0, c == CHUNKS - 1 and f == FT - 1)
                        last.then_inc(sem("f_wused"), 1)
                        continue
                    if kind == "g" and c >= 2:
                        pe.wait_ge(sem("f_hid"), c - 1)
                    for f in range(FT):
                        for k in range(KD):
                            if n == 0 and f == 0 and k % 4 == 0:
                                pe.wait_ge(sem("hl"), k // 4 + 1)
                            last = triple(ps[:, 2 * (c % 2) + (kind == "u"), f * SEQ:(f + 1) * SEQ],
                                          (n % SPLITS, k * FW + f * P), hh[:, k, :], hl[:, k, :], k == 0, k == KD - 1)
                    last.then_inc(sem("f_wused"), 1)
                residual_transposes(1)
                pe.wait_ge(sem("yg"), 2)
                ada_reduce(2)
                ada_reduce(3)

            def experts():
                for i in range(SPLITS):
                    mm(ps[:, 7, 0:1], ident[:, :], zero[:, 0:1], start=True, stop=True).then_inc(sem("w_used"), 1)
                norm_transposes(3)
                h_ready(3)
                pe.wait_ge(sem("consts"), 4)
                pe.wait_ge(sem("rw_in"), 16)
                for t in range(NT):
                    for k in range(KD):
                        last = mm(ps[:, 4, t * NE:(t + 1) * NE], hT[:, k, t * P:(t + 1) * P], rw[:, k, :],
                                  start=(k == 0), stop=(k == KD - 1))
                last.then_inc(sem("lg_ps"), 1)
                for t in range(NT):
                    for j in range(KD):
                        last = tr(ps[:, 2 * t + j // 4, (j % 4) * P:(j % 4 + 1) * P], hT[:, j, t * P:(t + 1) * P],
                                  ident[:, :])
                last.then_inc(sem("hnat_ps"), 1)
                pe.wait_ge(sem("chosen"), 1)
                mm(ps[:, 5, 0:NE], tri, rs[:, 0:NE], start=True, stop=True)
                mm(ps[:, 5, NE:2 * NE], ones[:, :], rs[:, 0:NE], start=True, stop=False)
                mm(ps[:, 5, NE:2 * NE], tri, rs[:, NE:2 * NE], start=False, stop=True)
                mm(ps[:, 5, 2 * NE:3 * NE], ones[:, :], rs[:, 0:NE], start=True, stop=False)
                mm(ps[:, 5, 2 * NE:3 * NE], ones[:, :], rs[:, NE:2 * NE], start=False, stop=True)\
                    .then_inc(sem("rank_ps"), 1)
                pe.wait_ge(sem("gate_cols"), 1)
                for j in range(KD):
                    last = mm(ps[:, 6 + j // 4, (j % 4) * P:(j % 4 + 1) * P], gate_cols[:, j, :], ident[:, :],
                              start=True, stop=True)
                last.then_inc(sem("gate_ps"), 1)
                pe.wait_ge(sem("hnat"), 2)
                pe.wait_ge(sem("meta"), 1)
                pe.wait_ge(sem("gate_row"), 1)
                gather(0)
                weights(0)
                passes = pe.value_load(meta[0:1, COUNT:COUNT + 1], min_val=NE, max_val=2 * NE)
                with pe.Fori(0, passes) as p:
                    one_pass(p)
                spread(passes, 0)
                spread(passes, 1)

            def gather(p):
                pe.wait_ge(sem("sel"), 2 * p + 1)
                mm(ps[:, 2, 0:1], ident[:, :], zero[:, 0:1], start=True, stop=True)
                for k in range(KD):
                    for t in range(NT):
                        last = mm(ps[:, 2 + k // 4, (k % 4) * P:(k % 4 + 1) * P], hnat[:, t, k * P:(k + 1) * P],
                                  sel[:, t, :], start=(t == 0), stop=(t == NT - 1))
                    if k % 4 == 3:
                        last.then_inc(sem("gath_ps"), 1)

            def weights(p):
                pe.wait_ge(sem("sel"), 2 * p + 2)
                mm(ps[:, 7, 0:1], ident[:, :], zero[:, 0:1], start=True, stop=True)
                for t in range(NT):
                    last = tr(ps[:, 7, t * P:(t + 1) * P], sel[:, t, :], ident[:, :])
                last.then_inc(sem("swT_ps"), 1)

            def spread(p, t):
                pe.wait_ge(sem("y_sb"), p + 1)
                if t == 0:
                    pe.wait_ge(sem("hT_lo"), 2 * p + 2)
                pe.wait_ge(sem("x_add"), 2 * p + t + 1)
                mm(ps[:, 2, 0:1], ident[:, :], zero[:, 0:1], start=True, stop=True)
                for half in range(2):
                    last = mm(ps[:, 2 + half, :], swT[:, t * P:(t + 1) * P], ynat[:, half * 512:(half + 1) * 512],
                              start=True, stop=True)
                last.then_inc(sem("spread_ps"), 1)

            def one_pass(p):
                def triple(out_, xh, xl, at, n, first, last_):
                    b, c0 = at
                    h, lo = wh[:, b, c0:c0 + n], wl[:, b, c0:c0 + n]
                    mm(out_, xh, h, start=first, stop=False, skip_group_check=True)
                    mm(out_, xh, lo, start=False, stop=False, skip_group_check=True)
                    return mm(out_, xl, h, start=False, stop=last_, skip_group_check=True)

                for j in range(HP):
                    kind, c = pieces[j // 2]
                    half = j % 2
                    if kind == "g" and c == 0:
                        pe.wait_ge(sem("hT_lo"), 2 * p + half + 1)
                    if kind == "g" and c == 1 and half == 0:
                        pe.wait_ge(sem("x_add"), 2 * p + 3)
                    if kind == "d" and half == 0:
                        pe.wait_ge(sem("fT_lo"), p * ECHUNKS + c + 1)
                    pe.wait_ge(sem("w_lo"), p * HP + j + 1)
                    if kind == "d":
                        for f in range(EFT // 2):
                            ff = half * EFT // 2 + f
                            for n in range(2):
                                last = triple(ps[:, 4 + n, :], *(x_[:, ff * P:(ff + 1) * P] for x_ in fT_parts(c)),
                                              (j % SPLITS, f * D + n * 512), 512, c == 0 and ff == 0,
                                              c == ECHUNKS - 1 and ff == EFT - 1)
                    else:
                        for k in range(KD // 2):
                            kk = half * KD // 2 + k
                            last = triple(ps[:, 2 * (c % 2) + (kind == "u"), :], hTh[:, kk, :], hTl[:, kk, :],
                                          (j % SPLITS, k * EW), EW, kk == 0, kk == KD - 1)
                    last.then_inc(sem("w_used"), 1)
                    if j in (0, 2):
                        spread(p, j // 2)
                    if j == GATHER_AFTER:
                        gather(p + 1)
                    if j in turn_after:
                        c = turn_after[j]
                        pe.wait_ge(sem("e_hid"), p * ECHUNKS + c + 1)
                        if c == 1:
                            pe.wait_ge(sem("swT"), p + 1)
                        for f in range(EFT):
                            last = tr(ps[:, 6 + c % 2, f * P:(f + 1) * P], e_hid[:, f * P:(f + 1) * P], ident[:, :])
                        last.then_inc(sem("fT_ps"), 1)
                    if j == SWT_AFTER:
                        weights(p + 1)

            pe.wait_ge(sem("consts"), 1)
            pe.wait_ge(sem("rowsA_in"), 16 * 9)
            pe.wait_ge(sem("rowsB_in"), 16)
            tr(ps[:, 0, 0:126], rowsA[0:126, :], ident[0:126, 0:126])
            tr(ps[:, 0, P:P + 96], rowsB[0:96, :], ident[0:96, 0:96]).then_inc(sem("cols_ps"), 1)
            pe.wait_ge(sem("cols_in"), 1)
            for l in range(DEPTH):
                mixer(l)
                if l == 0:
                    dense()
                else:
                    experts()

        @block.scalar
        def _(act):
            A = nc.scalar.activation
            r = rowsA
            s = sem("rowsA_in")
            act.dma_start(r[C0:C0 + 8, :], c_in[0].rearrange("(j p) -> j p", p=P)).then_inc(s, 16)
            act.dma_start(r[NG:NG + 32, :], norm_gain.rearrange("l s (j p) -> (l s j) p", p=P)).then_inc(s, 16)
            act.dma_start(rowsB[0:96, :], b_ada.rearrange("l s (j p) -> (l s j) p", p=P)).then_inc(sem("rowsB_in"), 16)
            act.dma_start(r[OG:OG + 16, :], out_gain.rearrange("l (j p) -> (l j) p", p=P)).then_inc(s, 16)
            act.dma_start(r[LG:LG + 6, :], latent_gain.rearrange("l (j p) -> (l j) p", p=P)).then_inc(s, 16)
            act.dma_start(r[CW:CW + 32, :], conv_w.rearrange("l w (j p) -> (l w j) p", p=P)).then_inc(s, 16)
            for at, v in ((CB, conv_b), (BA, b_a), (BX, b_x), (LM, lru_lambda)):
                act.dma_start(r[at:at + 8, :], v.rearrange("l (j p) -> (l j) p", p=P)).then_inc(s, 16)
            act.dma_start(pos_i[:, :], pos_in[0].rearrange("(t p) -> p t", p=P),
                          allow_slow_non_contiguous=True).then_inc(sem("pos_in"), 16)
            for l in range(DEPTH):
                for i, v in enumerate((q_gain, k_gain)):
                    act.dma_start(gains[:, 2 * l + i, :], v[l:l + 1, :].broadcast_to([P, QK]))\
                        .then_inc(sem("gains_in"), 16)
            act.dma_start(rw, router_w[0].rearrange("(k p) e -> p k e", p=P)).then_inc(sem("rw_in"), 16)

            act.wait_ge(sem("cols_in"), 1)
            A(cact[:, :], colA[:, C0:C0 + KD], ACT.Tanh, scale=0.5).then_inc(sem("a_set"), 1)
            A(m2ls[:, :], colA[:, LM:LM + 8], ACT.Abs).then_inc(sem("a_set"), 1)
            act.wait_ge(sem("a_set"), 2)
            A(m2ls[:, :], m2ls[:, :], ACT.Exp, scale=-1.0).then_inc(sem("a_set"), 1)
            act.wait_ge(sem("ang"), 1)
            A(cs.rearrange("p t i n -> p i t n"), ang, ACT.Sin).then_inc(sem("cs"), 1)

            roots = [0]

            def root(n):
                roots[0] += 1
                act.wait_ge(sem("ms"), roots[0])
                A(rs[:, 0:n], st[:, 0:n], ACT.Sqrt).then_inc(sem("root"), 1)

            def norm(n, meanwhile=None):
                if n == 0:
                    act.wait_ge(sem("x_in"), 16)
                else:
                    act.wait_ge(sem("x_new"), n)
                for t in range(NT):
                    A(xn[:, t, :], x[:, t, :], ACT.Square, accum_out=st[:, t:t + 1]).then_inc(sem("ss_n"), 1)
                root(NT)
                if meanwhile:
                    meanwhile()
                act.wait_ge(sem("xT_ps"), n + 1)
                act.wait_ge(sem("mod"), n + 1)
                for j in range(KD // 2):
                    last = A(hT[:, j, :], ps[:, j // 2, (j % 2) * SEQ:(j % 2 + 1) * SEQ], ACT.Identity,
                             bias=adav[:, n, j:j + 1], scale=adaA[:, n, j:j + 1])
                last.then_inc(sem("hT_act"), 1)

            def gate_evac(n):
                for j in range(KD // 2):
                    last = A(ygT[:, j, :], ps[:, 4 + j // 2, (j % 2) * SEQ:(j % 2 + 1) * SEQ], ACT.Copy,
                             scale=adav[:, n, 16 + j:17 + j])
                last.then_inc(sem("yg_a"), 1)

            def mixer(l):
                norm(2 * l)
                for t in range(NT):
                    act.wait_ge(sem("lat_ps"), 2 * l + t + 1)
                    for i, (a, b) in enumerate(((0, Q_RANK), (Q_RANK, Q_RANK + KV_RANK), (Q_RANK + KV_RANK, LAT))):
                        last = A(cn[:, t, a:b], ps[:, 4 + t, a:b], ACT.Square, accum_out=st[:, 3 * t + i:3 * t + i + 1])
                last.then_inc(sem("ss_l"), 1)
                root(3 * NT)
                act.wait_ge(sem("pad"), l + 1)
                act.wait_ge(sem("rec_ps"), 2 * l + 1)
                A(xp[:, :, TAPS - 1:], bank2(6).rearrange("p (i n) -> p i n", i=LT), ACT.Copy).then_inc(sem("xp"), 1)
                act.wait_ge(sem("rec_ps"), 2 * l + 2)
                A(gr, bank2(0).rearrange("p (i n) -> p i n", i=LT), ACT.Copy).then_inc(sem("rec_sb"), 1)
                act.wait_ge(sem("rec_sb"), l + 1)
                A(lq, gr, ACT.Square).then_inc(sem("g_sq"), 1)
                for t, (bq, bk) in enumerate(((4, 2), (6, 0))):
                    act.wait_ge(sem("up_ps"), 2 * l + t + 1)
                    if t or l:
                        act.wait_ge(sem("sq_used"), 2 * (2 * l + t))
                    else:
                        act.wait_ge(sem("cT_ps"), 1)
                    for half in range(2):
                        A(sq[:, half * 384:(half + 1) * 384], ps[:, bq + half, 0:384], ACT.Square)\
                            .then_inc(sem("q_sq"), 1)
                    act.wait_ge(sem("sq_used"), 2 * (2 * l + t) + 1)
                    for half in range(2):
                        kvb = ps[:, bk + half, :].rearrange("p (h n) -> p h n", h=H // 2)
                        A(sq[:, half * 256:(half + 1) * 256].rearrange("p (h n) -> p h n", h=H // 2),
                          kvb[:, :, 0:NOPE], ACT.Square).then_inc(sem("k_sq"), 1)
                    for half in range(2):
                        kvb = ps[:, bk + half, :].rearrange("p (h n) -> p h n", h=H // 2)
                        last = A(v_sb[:, t, half * 256:(half + 1) * 256].rearrange("p (h n) -> p h n", h=H // 2),
                                 kvb[:, :, NOPE:NOPE + V], ACT.Copy)
                    last.then_inc(sem("v"), 1)
                    root(24)
                act.wait_ge(sem("g_arg"), l + 1)
                A(lq, lq, ACT.Tanh, scale=GELU_B).then_inc(sem("g_tanh"), 1)
                for t, bq in enumerate((4, 6)):
                    act.wait_ge(sem("qkT_ps"), 2 * l + t + 1)
                    for half in range(2):
                        last = A(qT[0:QK, 4 * half:4 * half + 4, t * P:(t + 1) * P],
                                 ps[0:QK, bq + half, :].rearrange("p (h n) -> p h n", h=4), ACT.Copy)
                    last.then_inc(sem("qT"), 1)
                act.wait_ge(sem("rg_ps"), l + 1)
                for g, (b0, dst) in enumerate(((6, la), (0, li))):
                    for i in range(LT):
                        last = A(dst[:, i, :], ps[:, b0 + i // 2, (i % 2) * SEQ:(i % 2 + 1) * SEQ], ACT.Tanh,
                                 bias=hb[:, g * 8 + l * LT + i:g * 8 + l * LT + i + 1], scale=0.5)
                last.then_inc(sem("rg"), 1)
                act.wait_ge(sem("rg"), l + 1)
                for i in range(LT):
                    m = m2ls[:, l * LT + i:l * LT + i + 1]
                    last = A(la[:, i, :], la[:, i, :], ACT.Tanh, bias=m, scale=m)
                last.then_inc(sem("lt"), 1)
                for n, (buf, keys) in enumerate(((s1, SEQ), (s0, P))):
                    act.wait_ge(sem("nmax"), 2 * l + n + 1)
                    for h in range(H):
                        last = A(buf[:, h, :], buf[:, h, :], ACT.Exp, bias=mx[:, n * H + h:n * H + h + 1],
                                 scale=SCALE, accum_out=den[:, n * H + h:n * H + h + 1])
                    last.then_inc(sem("p"), 1)
                act.wait_ge(sem("pT_ps"), 2 * l + 1)
                A(PT[:, 1, :, :].rearrange("p h n -> p (h n)"), bank2(2), ACT.Copy).then_inc(sem("pT_a"), 1)
                act.wait_ge(sem("pT_ps"), 2 * l + 2)
                A(PT[:, 0, :, :].rearrange("p h n -> p (h n)"), bank2(0), ACT.Copy).then_inc(sem("pT_a"), 1)
                act.wait_ge(sem("lq_free"), l + 1)
                A(lq, la, ACT.Sqrt).then_inc(sem("lroot"), 1)
                act.wait_ge(sem("rec"), l + 1)
                A(la, lx, ACT.Square).then_inc(sem("recsq"), 1)
                act.wait_ge(sem("o_sb"), l + 1)
                for t in range(NT):
                    last = A(PT[:, t, 0:H // 2, :].rearrange("p h n -> p (h n)"),
                             osb[:, t, :, :].rearrange("p h n -> p (h n)"), ACT.Square,
                             accum_out=st[:, t:t + 1])
                last.then_inc(sem("ss_o"), 1)
                root(NT)
                act.wait_ge(sem("rbc_ms"), l + 1)
                A(rbc, rbc, ACT.Sqrt).then_inc(sem("rbc_root"), 1)
                act.wait_ge(sem("onT_ps"), l + 1)
                for i in range(2):
                    last = A(mT[:, i, :], ps[:, 0, i * SEQ:(i + 1) * SEQ], ACT.Copy,
                             scale=colA[:, OG + 8 * l + i:OG + 8 * l + i + 1])
                last.then_inc(sem("mT_a"), 1)
                act.wait_ge(sem("wout_done"), l + 1)
                gate_evac(2 * l)

            def dense():
                def high(n):
                    kind, c = units[n]
                    act.wait_ge(sem(f"ffn_{kind}{c % 3}_in"), 16 * (c // 3 + 1))
                    if n >= SPLITS:
                        act.wait_ge(sem("f_wused"), n - SPLITS + 1)
                    A(wh[:, n % SPLITS, :], unit(kind, c), ACT.Copy).then_inc(sem("f_hi"), 1)

                norm(1, lambda: high(0))
                for half, ready in enumerate(("hT_act", "hT_dve")):
                    act.wait_ge(sem(ready), 2)
                    A(hh[:, 4 * half:4 * half + 4, :], hT[:, 4 * half:4 * half + 4, :], ACT.Copy)\
                        .then_inc(sem("hh"), 1)
                high(1)
                high(2)
                for n, (kind, c) in enumerate(units):
                    if kind == "u":
                        act.wait_ge(sem("f_wused"), n + 1)
                        A(f_tg, ps[:, 2 * (c % 2), :], ACT.Tanh, scale=0.5).then_inc(sem("f_tanh"), 1)
                        act.wait_ge(sem("f_hid"), c + 1)
                        A(fh[:, c % 2, :], f_hid, ACT.Copy).then_inc(sem("fh"), 1)
                    if n + SPLITS < len(units):
                        high(n + SPLITS)
                act.wait_ge(sem("f_wused"), len(units))
                gate_evac(1)

            def experts():
                norm(3, lambda: [high(0, j) for j in range(SPLITS)])
                act.wait_ge(sem("hnat_ps"), 1)
                A(hnat[:, 0, :], bank2(0), ACT.Copy).then_inc(sem("hnat"), 1)
                act.wait_ge(sem("w_dif"), 1)
                A(st[:, 8:10], st[:, 8:10], ACT.Exp).then_inc(sem("w_exp"), 1)
                act.wait_ge(sem("gate_ps"), 1)
                A(gate_row, bank2(6), ACT.Copy).then_inc(sem("gate_row"), 1)
                act.wait_ge(sem("meta"), 1)
                passes = act.value_load(meta[0:1, COUNT:COUNT + 1], min_val=NE, max_val=2 * NE)
                high_h(0)
                with act.Fori(0, passes) as p:
                    one_pass(p)

            def high(p, j):
                i = j // 2
                n = NP // SLOTS * p + i // SLOTS + 1
                act.wait_ge(sem(f"piece{piece_slot(i)}_in"), 16 * n)
                act.wait_ge(sem("w_used"), p * HP + j + 1)
                A(wh[:, j % SPLITS, :], piece_half(j), ACT.Copy).then_inc(sem("w_hi"), 1)

            def high_h(p):
                for half in range(2):
                    act.wait_ge(sem("gath_ps"), 2 * p + half + 1)
                    A(hTh[:, half * 4:half * 4 + 4, :].rearrange("p k n -> p (k n)"), ps[:, 2 + half, :], ACT.Copy)\
                        .then_inc(sem("hT_hi"), 1)

            def one_pass(p):
                for j in range(HP):
                    if j == 3:
                        act.wait_ge(sem("spread_ps"), 2 * p + 2)
                        act.wait_ge(sem("swT_ps"), p + 1)
                        A(swT, ps[:, 7, 0:NT * P], ACT.Copy).then_inc(sem("swT"), 1)
                    if j in silu_after:
                        c = silu_after[j]
                        act.wait_ge(sem("w_used"), p * HP + j + 1 + SPLITS)
                        A(e_tg, ps[:, 2 * (c % 2), :], ACT.Tanh, scale=0.5).then_inc(sem("e_tanh"), 1)
                    if j in turn_after:
                        act.wait_ge(sem("fT_ps"), p * ECHUNKS + turn_after[j] + 1)
                        A(fT_parts(turn_after[j])[0], ps[:, 6 + turn_after[j] % 2, :], ACT.Copy)\
                            .then_inc(sem("fT_hi"), 1)
                    if j == SPLIT_H_AFTER:
                        high_h(p + 1)
                    high(p, j + SPLITS)

            for l in range(DEPTH):
                mixer(l)
                if l == 0:
                    dense()
                else:
                    experts()

        @block.vector
        def _(dve):
            v = nc.vector
            chain = [0]

            def link(ins):
                chain[0] += 1
                ins.then_inc(sem("dve"), 1)
                dve.wait_ge(sem("dve"), chain[0])

            roots = [0]

            def rstd(n, inv):
                roots[0] += 1
                v.tensor_scalar(st[:, 0:n], st[:, 0:n], inv, EPS, ALU.mult, ALU.add).then_inc(sem("ms"), 1)
                dve.wait_ge(sem("root"), roots[0])
                link(v.reciprocal(rs[:, 0:n], rs[:, 0:n]))

            def normalise(n):
                dve.wait_ge(sem("ss_n"), 2 * (n + 1))
                rstd(NT, 1.0 / D)
                if n == 0:
                    dve.wait_ge(sem("x_in"), 16)
                for t in range(NT):
                    last = v.tensor_scalar(xn[:, t, :], x[:, t, :], rs[:, t:t + 1], None, ALU.mult)
                last.then_inc(sem("xn"), 1)

            dve.wait_ge(sem("cols_ps"), 1)
            v.tensor_copy(colA[:, :], ps[:, 0, 0:126])
            v.tensor_copy(colB[:, :], ps[:, 0, P:P + 96]).then_inc(sem("cols_in"), 1)
            dve.wait_ge(sem("cols_in"), 1)
            link(v.tensor_scalar(hb[:, :], colA[:, BA:BA + 16], 0.5, None, ALU.mult))
            dve.wait_ge(sem("a_set"), 3)
            link(v.tensor_scalar(cact[:, :], cact[:, :], 0.5, 0.5, ALU.mult, ALU.add))
            link(v.tensor_tensor(cact[:, :], cact[:, :], colA[:, C0:C0 + KD], ALU.mult))
            v.tensor_copy(mark[:, 4:5], cact[:, 0:1]).then_inc(sem("setup"), 1)

            prev = None
            for i in range(KD):
                w = place(wait_fill(dve, "ada", 0, i), 3 * D)
                if prev is None:
                    last = v.tensor_scalar(w, w, cact[:, 0:1], None, ALU.mult)
                else:
                    last = v.scalar_tensor_tensor(out=w, in0=w, scalar=cact[:, i:i + 1], in1=prev, op0=ALU.mult,
                                                  op1=ALU.add)
                last.then_inc(sem("ada_step0"), 1)
                dve.wait_ge(sem("ada_step0"), i + 1)
                prev = w
                if i == 0:
                    z, z2, pz = st[:, 0:8], st[:, 8:16], st[:, 16:24]
                    link(v.tensor_scalar(z, m2ls[:, :], 2.0, None, ALU.add))
                    link(v.reciprocal(z, z))
                    link(v.tensor_tensor(z, z, m2ls[:, :], ALU.mult))
                    link(v.tensor_tensor(z2, z, z, ALU.mult))
                    link(v.tensor_scalar(pz, z2, 1.0 / 17.0, None, ALU.mult))
                    for k in range(7, 0, -1):
                        link(v.scalar_tensor_tensor(out=pz, in0=pz, scalar=1.0 / (2 * k + 1), in1=z2, op0=ALU.add,
                                                    op1=ALU.mult))
                    link(v.scalar_tensor_tensor(out=pz, in0=pz, scalar=1.0, in1=z, op0=ALU.add, op1=ALU.mult))
                    link(v.tensor_scalar(z, colA[:, LM:LM + 8], 0.0, -2.0, ALU.min, ALU.mult))
                    link(v.scalar_tensor_tensor(out=m2ls[:, :], in0=pz, scalar=4.0, in1=z, op0=ALU.mult, op1=ALU.add))
                if i == 1:
                    c1, c2, c3 = cody_waite()
                    dve.wait_ge(sem("pos_in"), 16)
                    dve.wait_ge(sem("consts"), 4)
                    link(v.tensor_copy(pos_f[:, :], pos_i[:, :]))
                    for j in range(2):
                        for t in range(NT):
                            link(v.tensor_scalar(ang[:, j, t, :], ivf, pos_f[:, t:t + 1], None, ALU.mult))
                        magic = 1.5 * 2.0 ** 23
                        link(v.tensor_scalar(angk[:, j, :, :], ang[:, j, :, :], 1.0 / TWO_PI, 0.25 if j == 0 else 0.0,
                                             ALU.mult, ALU.add))
                        link(v.tensor_scalar(angk[:, j, :, :], angk[:, j, :, :], magic, None, ALU.add))
                        link(v.tensor_scalar(angk[:, j, :, :], angk[:, j, :, :], -magic, None, ALU.add))
                        for c in (c1, c2, c3):
                            link(v.scalar_tensor_tensor(out=ang[:, j, :, :], in0=angk[:, j, :, :], scalar=-c,
                                                        in1=ang[:, j, :, :], op0=ALU.mult, op1=ALU.add))
                        if j == 0:
                            link(v.tensor_scalar(ang[:, j, :, :], ang[:, j, :, :], float(np.pi / 2), None, ALU.add))
                        link(v.tensor_scalar(ang[:, j, :, :], ang[:, j, :, :], -3.1415925, 3.1415925, ALU.max, ALU.min))
                    v.tensor_copy(mark[:, 5:6], cact[:, 0:1]).then_inc(sem("ang"), 1)
                if i == 2:
                    dve.wait_ge(sem("cs"), 1)
                    v.tensor_copy(mark[:, 6:7], cact[:, 0:1]).then_inc(sem("setup"), 1)
                if i == 3:
                    normalise(0)

            def norm(n, meanwhile=None):
                if n:
                    normalise(n)
                for a in ((0,), (1,), (2, 3), ())[n]:
                    dve.wait_ge(sem("ada_red"), a + 1)
                    link(v.tensor_tensor(adav[:, a, :], ps[:, 4 + (a == 3), 0:24], colB[:, 24 * a:24 * a + 24],
                                         ALU.add))
                    v.scalar_tensor_tensor(out=adaA[:, a, :], in0=adav[:, a, 8:16], scalar=1.0,
                                           in1=colA[:, NG + 8 * a:NG + 8 * a + 8], op0=ALU.add, op1=ALU.mult)\
                        .then_inc(sem("mod"), 1)
                if meanwhile:
                    meanwhile()
                dve.wait_ge(sem("xT_ps"), n + 1)
                dve.wait_ge(sem("mod"), n + 1)
                for j in range(KD // 2, KD):
                    last = v.tensor_scalar(hT[:, j, :], ps[:, j // 2, (j % 2) * SEQ:(j % 2 + 1) * SEQ],
                                           adaA[:, n, j:j + 1], adav[:, n, j:j + 1], ALU.mult, ALU.add)
                last.then_inc(sem("hT_dve"), 1)

            def residual(n):
                for j in range(KD // 2, KD):
                    last = v.tensor_scalar(ygT[:, j, :], ps[:, 4 + j // 2, (j % 2) * SEQ:(j % 2 + 1) * SEQ],
                                           adav[:, n, 16 + j:17 + j], None, ALU.mult)
                link(last)
                dve.wait_ge(sem("yg_a"), n + 1)
                v.tensor_copy(mark[:, 7:8], cact[:, 0:1]).then_inc(sem("yg"), 1)
                dve.wait_ge(sem("res_ps"), n + 1)
                for t in range(NT):
                    last = v.tensor_tensor(x[:, t, :], x[:, t, :], bank2(2 * t), ALU.add)
                last.then_inc(sem("x_new"), 1)
                dve.wait_ge(sem("x_new"), n + 1)

            def bc(col, n):
                return col.unsqueeze(2).broadcast_to([P, col.shape[1], n])

            def rope(dst, src, t, heads):
                cos = cs[:, t, 0:1, :].broadcast_to([P, heads, HALF])
                sin = cs[:, t, 1:2, :].broadcast_to([P, heads, HALF])
                x1, x2 = src[:, :, 0:HALF], src[:, :, HALF:ROPE]
                tmp = [rope_tmp[:, i, 0:heads, :] for i in range(4)]
                v.tensor_tensor(tmp[0], x1, cos, ALU.mult)
                v.tensor_tensor(tmp[1], x2, sin, ALU.mult)
                v.tensor_tensor(tmp[2], x1, sin, ALU.mult)
                link(v.tensor_tensor(tmp[3], x2, cos, ALU.mult))
                v.tensor_tensor(dst[:, :, 0:HALF], tmp[0], tmp[1], ALU.subtract)
                link(v.tensor_tensor(dst[:, :, HALF:ROPE], tmp[2], tmp[3], ALU.add))

            def mixer(l):
                norm(2 * l)
                dve.wait_ge(sem("ss_l"), l + 1)
                for t in range(NT):
                    for i, w in enumerate((Q_RANK, KV_RANK, ROPE)):
                        c = 3 * t + i
                        last = v.tensor_scalar(st[:, c:c + 1], st[:, c:c + 1], 1.0 / w, EPS, ALU.mult, ALU.add)
                roots[0] += 1
                last.then_inc(sem("ms"), 1)
                dve.wait_ge(sem("root"), roots[0])
                link(v.reciprocal(rs[:, 0:6], rs[:, 0:6]))
                for t in range(NT):
                    for i, (a, b) in enumerate(((0, Q_RANK), (Q_RANK, Q_RANK + KV_RANK), (Q_RANK + KV_RANK, LAT))):
                        last = v.tensor_scalar(cn[:, t, a:b], ps[:, 4 + t, a:b], rs[:, 3 * t + i:3 * t + i + 1], None,
                                               ALU.mult)
                last.then_inc(sem("cn"), 1)
                dve.wait_ge(sem("cn"), l + 1)
                if l == 0:
                    dve.wait_ge(sem("gains_in"), 64)
                for t in range(NT):
                    kr = cn[:, t, Q_RANK + KV_RANK:LAT]
                    link(v.tensor_tensor(kr, kr, gains[:, 2 * l + 1, NOPE:QK], ALU.mult))
                    rope(kn[:, t, 0:1, NOPE:QK], kr.unsqueeze(1), t, 1)
                    v.tensor_copy(kn[:, t, 1:H, NOPE:QK], kn[:, t, 0:1, NOPE:QK].broadcast_to([P, H - 1, ROPE]))
                dve.wait_ge(sem("cT_ps"), l + 1)
                for i in range(3):
                    last = v.tensor_scalar(cT[:, i, :], ps[:, 2 + i // 2, (i % 2) * SEQ:(i % 2 + 1) * SEQ],
                                           colA[:, LG + 3 * l + i:LG + 3 * l + i + 1], None, ALU.mult)
                last.then_inc(sem("cT"), 1)
                dve.wait_ge(sem("xp"), l + 1)
                for w in range(TAPS):
                    for i in range(LT):
                        col = colA[:, CW + 16 * l + 4 * w + i:CW + 16 * l + 4 * w + i + 1]
                        src = xp[:, i, w:w + SEQ]
                        if w == 0:
                            last = v.tensor_scalar(lx[:, i, :], src, col, colA[:, CB + 4 * l + i:CB + 4 * l + i + 1],
                                                   ALU.mult, ALU.add)
                        else:
                            last = v.scalar_tensor_tensor(out=lx[:, i, :], in0=src, scalar=col, in1=lx[:, i, :],
                                                          op0=ALU.mult, op1=ALU.add)
                    if w < TAPS - 1:
                        link(last)
                last.then_inc(sem("xr"), 1)
                dve.wait_ge(sem("xr"), l + 1)
                for t, (bq, bk) in enumerate(((4, 2), (6, 0))):
                    n = 2 * l + t
                    dve.wait_ge(sem("q_sq"), 2 * (n + 1))
                    sqq = sq[:, 0:H * QK].rearrange("p (h n) -> p h n", h=H)
                    v.tensor_reduce(st[:, 0:H], sqq[:, :, 0:NOPE], AX, ALU.add)
                    v.tensor_reduce(st[:, H:2 * H], sqq[:, :, NOPE:QK], AX, ALU.add).then_inc(sem("sq_used"), 1)
                    dve.wait_ge(sem("k_sq"), 2 * (n + 1))
                    v.tensor_reduce(st[:, 2 * H:3 * H], sq[:, 0:H * NOPE].rearrange("p (h n) -> p h n", h=H), AX,
                                    ALU.add).then_inc(sem("sq_used"), 1)
                    dve.wait_ge(sem("sq_used"), 2 * (n + 1))
                    link(v.tensor_scalar(st[:, H:2 * H], st[:, H:2 * H], float(NOPE) / ROPE, None, ALU.mult))
                    rstd(3 * H, 1.0 / NOPE)
                    dve.wait_ge(sem("v"), n + 1)
                    for half in range(2):
                        hs = slice(4 * half, 4 * half + 4)
                        qb = ps[:, bq + half, 0:4 * QK].rearrange("p (h n) -> p h n", h=4)
                        kb = ps[:, bk + half, :].rearrange("p (h n) -> p h n", h=4)
                        v.tensor_tensor(qn[:, t, hs, 0:NOPE], qb[:, :, 0:NOPE],
                                        bc(rs[:, 4 * half:4 * half + 4], NOPE), ALU.mult)
                        v.tensor_tensor(qn[:, t, hs, NOPE:QK], qb[:, :, NOPE:QK],
                                        bc(rs[:, H + 4 * half:H + 4 * half + 4], ROPE), ALU.mult)
                        last = v.tensor_tensor(kn[:, t, hs, 0:NOPE], kb[:, :, 0:NOPE],
                                               bc(rs[:, 2 * H + 4 * half:2 * H + 4 * half + 4], NOPE), ALU.mult)
                    link(last)
                    link(v.tensor_tensor(qn[:, t, :, :], qn[:, t, :, :],
                                         gains[:, 2 * l:2 * l + 1, :].broadcast_to([P, H, QK]), ALU.mult))
                    v.tensor_tensor(kn[:, t, :, 0:NOPE], kn[:, t, :, 0:NOPE],
                                    gains[:, 2 * l + 1:2 * l + 2, 0:NOPE].broadcast_to([P, H, NOPE]), ALU.mult)
                    rope(qn[:, t, :, NOPE:QK], qn[:, t, :, NOPE:QK], t, H)
                    v.tensor_copy(mark[:, 8:9], cact[:, 0:1]).then_inc(sem("qk"), 1)
                    if t == 0:
                        dve.wait_ge(sem("g_sq"), l + 1)
                        link(v.tensor_scalar(lq, lq, GELU_A, 1.0, ALU.mult, ALU.add))
                        v.tensor_tensor(lq, lq, gr, ALU.mult).then_inc(sem("g_arg"), 1)
                for t, bk in enumerate((2, 0)):
                    dve.wait_ge(sem("qkT_ps"), 2 * l + t + 1)
                    for half in range(2):
                        last = v.tensor_copy(kT[0:QK, 4 * half:4 * half + 4, t * P:(t + 1) * P],
                                             ps[0:QK, bk + half, :].rearrange("p (h n) -> p h n", h=4))
                    last.then_inc(sem("kT"), 1)
                dve.wait_ge(sem("g_tanh"), l + 1)
                v.scalar_tensor_tensor(out=gr, in0=lq, scalar=1.0, in1=gr, op0=ALU.add, op1=ALU.mult)\
                    .then_inc(sem("lq_free"), 1)
                for n, (buf, keys, b0, nb) in enumerate(((s1, SEQ, 2, 4), (s0, P, 0, 2))):
                    dve.wait_ge(sem("s_ps"), 2 * l + n + 1)
                    m = mask[:, SEQ - keys:SEQ].unsqueeze(1).broadcast_to([P, H, keys])
                    link(v.tensor_tensor(buf, bank2(b0, nb).rearrange("p (h n) -> p h n", h=H), m, ALU.add))
                    link(v.tensor_reduce(mx[:, n * H:(n + 1) * H], buf, AX, ALU.max))
                    v.tensor_scalar(mx[:, n * H:(n + 1) * H], mx[:, n * H:(n + 1) * H], -SCALE, None, ALU.mult)\
                        .then_inc(sem("nmax"), 1)
                dve.wait_ge(sem("lt"), l + 1)
                link(v.scalar_tensor_tensor(out=li, in0=li, scalar=1.0, in1=lx, op0=ALU.add, op1=ALU.mult))
                link(v.tensor_scalar(lr, la, 1.0, None, ALU.add))
                link(v.reciprocal(lr, lr))
                dve.wait_ge(sem("pT_ps"), 2 * l + 1)
                v.tensor_copy(PT[:, 2, :, :].rearrange("p h n -> p (h n)"), bank2(4)).then_inc(sem("pT_d"), 1)
                dve.wait_ge(sem("lroot"), l + 1)
                link(v.tensor_tensor(li, li, lr, ALU.mult))
                link(v.tensor_tensor(li, li, lq, ALU.mult))
                link(v.tensor_scalar(la, la, -1.0, 1.0, ALU.mult, ALU.add))
                link(v.tensor_tensor(la, la, lr, ALU.mult))
                for i in range(LT):
                    last = v.tensor_tensor_scan(lq[:, i, :], la[:, i, :], li[:, i, :], 0.0, ALU.mult, ALU.add)
                link(last)
                v.scalar_tensor_tensor(out=lx, in0=lq, scalar=0.5, in1=gr, op0=ALU.mult, op1=ALU.mult)\
                    .then_inc(sem("rec"), 1)
                link(v.reciprocal(den[:, :], den[:, :]))
                for n, t in enumerate((1, 0)):
                    dve.wait_ge(sem("o_ps"), 2 * l + n + 1)
                    last = v.tensor_tensor(osb[:, t, :, :], ps[:, 6 + t, :].rearrange("p (h n) -> p h n", h=H),
                                           bc(den[:, n * H:(n + 1) * H], V), ALU.mult)
                last.then_inc(sem("o_sb"), 1)
                dve.wait_ge(sem("ss_o"), l + 1)
                rstd(NT, 1.0 / (H * V))
                for t in range(NT):
                    o = osb[:, t, :, :].rearrange("p h n -> p (h n)")
                    last = v.tensor_scalar(o, o, rs[:, t:t + 1], None, ALU.mult)
                last.then_inc(sem("on"), 1)
                dve.wait_ge(sem("rss_ps"), l + 1)
                v.tensor_scalar(rbc, ps[:, 2, 0:SEQ], 1.0 / LRU, EPS, ALU.mult, ALU.add).then_inc(sem("rbc_ms"), 1)
                dve.wait_ge(sem("rbc_root"), l + 1)
                link(v.reciprocal(rbc, rbc))
                for i in range(LT):
                    v.scalar_tensor_tensor(out=mT[:, LT + i, :], in0=lx[:, i, :],
                                           scalar=colA[:, OG + 8 * l + LT + i:OG + 8 * l + LT + i + 1], in1=rbc,
                                           op0=ALU.mult, op1=ALU.mult)
                dve.wait_ge(sem("onT_ps"), l + 1)
                for i in range(2, LT):
                    last = v.tensor_scalar(mT[:, i, :], ps[:, 1, (i - 2) * SEQ:(i - 1) * SEQ],
                                           colA[:, OG + 8 * l + i:OG + 8 * l + i + 1], None, ALU.mult)
                link(last)
                dve.wait_ge(sem("mT_a"), l + 1)
                v.tensor_copy(mark[:, 9:10], cact[:, 0:1]).then_inc(sem("mT"), 1)
                dve.wait_ge(sem("wout_done"), l + 1)
                residual(2 * l)

            def dense():
                def low(n):
                    dve.wait_ge(sem("f_hi"), n + 1)
                    if n in (1, 2):
                        dve.wait_ge(sem("ada_step1"), 15)
                    v.tensor_tensor(wl[:, n % SPLITS, :], unit(*units[n]), wh[:, n % SPLITS, :].bitcast(F32),
                                    ALU.subtract).then_inc(sem("f_lo"), 1)

                norm(1, lambda: low(0))
                dve.wait_ge(sem("hT_dve"), 2)
                for half in range(2):
                    hs = slice(4 * half, 4 * half + 4)
                    dve.wait_ge(sem("hh"), half + 1)
                    v.tensor_tensor(hl[:, hs, :], hT[:, hs, :], hh[:, hs, :].bitcast(F32), ALU.subtract)\
                        .then_inc(sem("hl"), 1)
                low(1)
                low(2)
                for n, (kind, c) in enumerate(units):
                    if kind == "u":
                        dve.wait_ge(sem("f_tanh"), c + 1)
                        b = 2 * (c % 2)
                        link(v.scalar_tensor_tensor(out=f_tg, in0=f_tg, scalar=1.0, in1=ps[:, b, :], op0=ALU.add,
                                                    op1=ALU.mult))
                        v.scalar_tensor_tensor(out=f_hid, in0=f_tg, scalar=0.5, in1=ps[:, b + 1, :], op0=ALU.mult,
                                               op1=ALU.mult).then_inc(sem("f_hid"), 1)
                        dve.wait_ge(sem("fh"), c + 1)
                        v.tensor_tensor(fl[:, c % 2, :], f_hid, fh[:, c % 2, :].bitcast(F32), ALU.subtract)\
                            .then_inc(sem("fl"), 1)
                    if n + SPLITS < len(units):
                        low(n + SPLITS)
                dve.wait_ge(sem("f_wused"), len(units))
                residual(1)

            def experts():
                norm(3, lambda: low(0, 0))
                for j in range(KD):
                    last = v.tensor_scalar(gate_cols[:, j, :], ones[:, :], adav[:, 3, 16 + j:17 + j], None, ALU.mult)
                last.then_inc(sem("gate_cols"), 1)
                low(0, 1)
                low(0, 2)
                dve.wait_ge(sem("lg_ps"), 1)
                lg = st[:, 16:32]
                link(v.tensor_copy(lg, ps[:, 4, 0:NT * NE]))
                for t in range(NT):
                    top = part(F, 2560 + 64 * t, 8)
                    idx = part(F, 2568 + 64 * t, 8).bitcast(U32)
                    idf = part(F, 2576 + 64 * t, 8)
                    one = part(F, 2584 + 64 * t, 2, 8)
                    mine = lg[:, t * NE:(t + 1) * NE]
                    link(v.max(top, mine))
                    link(v.max_index(idx, top, mine))
                    link(v.tensor_copy(idf, idx))
                    for r in range(2):
                        link(v.tensor_scalar(one[:, r, :], iota[:, 0:NE], idf[:, r:r + 1], None, ALU.is_equal))
                    link(v.tensor_tensor(st[:, 8 + t:9 + t], top[:, 1:2], top[:, 0:1], ALU.subtract))
                    last = v.tensor_tensor(rs[:, t * NE:(t + 1) * NE], one[:, 0, :], one[:, 1, :], ALU.add)
                    link(last)
                v.tensor_copy(mark[:, 10:11], cact[:, 0:1]).then_inc(sem("chosen"), 1)
                v.tensor_copy(mark[:, 11:12], cact[:, 0:1]).then_inc(sem("w_dif"), 1)
                dve.wait_ge(sem("hnat_ps"), 1)
                v.tensor_copy(hnat[:, 1, :], bank2(2)).then_inc(sem("hnat"), 1)
                dve.wait_ge(sem("w_exp"), 1)
                link(v.tensor_scalar(st[:, 10:12], st[:, 8:10], 1.0, None, ALU.add))
                link(v.reciprocal(st[:, 10:12], st[:, 10:12]))
                link(v.tensor_tensor(st[:, 8:10], st[:, 8:10], st[:, 10:12], ALU.mult))
                for t in range(NT):
                    one = part(F, 2584 + 64 * t, 2, 8)
                    link(v.tensor_scalar(one[:, 1, :], one[:, 1, :], st[:, 8 + t:9 + t], None, ALU.mult))
                    link(v.scalar_tensor_tensor(out=wts[:, t, :], in0=one[:, 0, :], scalar=st[:, 10 + t:11 + t],
                                                in1=one[:, 1, :], op0=ALU.mult, op1=ALU.add))
                dve.wait_ge(sem("rank_ps"), 1)
                pm = posm.rearrange("p t e -> p (t e)")
                link(v.scalar_tensor_tensor(out=pm, in0=ps[:, 5, 0:NT * NE], scalar=1.0, in1=rs[:, 0:NT * NE],
                                            op0=ALU.add, op1=ALU.mult))
                link(v.tensor_scalar(pm, pm, -1.0, None, ALU.add))
                cnt = part(F, 2700, NE)
                tmp = part(F, 2708, NE)
                inc = part(F, 2716, NE)
                per = part(F, 2724, NE)
                link(v.tensor_copy(cnt, ps[:, 5, 2 * NE:3 * NE]))
                link(v.tensor_scalar(per, cnt, float(P), 1.0, ALU.is_gt, ALU.add))
                link(v.tensor_scalar(tmp, per, 0.0, 1.0, ALU.mult, ALU.add))
                link(v.tensor_tensor_scan(inc, tmp, per, 0.0, ALU.mult, ALU.add))
                link(v.tensor_copy(meta[:, COUNT:], inc[:, NE - 1:NE]))
                link(v.tensor_tensor(inc, inc, per, ALU.subtract))
                started = part(F, 2732, TABLE, NE)
                starts = part(F, 2872, TABLE, NE)
                pass_of = iota[:, 0:TABLE].unsqueeze(2).broadcast_to([P, TABLE, NE])
                link(v.tensor_tensor(started, inc.unsqueeze(1).broadcast_to([P, TABLE, NE]), pass_of, ALU.is_le))
                link(v.tensor_tensor(starts, started, inc.unsqueeze(1).broadcast_to([P, TABLE, NE]), ALU.mult))
                expert_of = part(F, 3012, TABLE)
                first_of = part(F, 3032, TABLE)
                link(v.tensor_reduce(expert_of, started, AX, ALU.add))
                link(v.tensor_reduce(first_of, starts, AX, ALU.max))
                link(v.tensor_scalar(expert_of, expert_of, -1.0, None, ALU.add))
                link(v.tensor_tensor(first_of, iota[:, 0:TABLE], first_of, ALU.subtract))
                link(v.tensor_scalar(first_of, first_of, 1.0, None, ALU.min))
                link(v.tensor_copy(meta[:, 0:TABLE], expert_of))
                link(v.tensor_copy(meta[:, TABLE:COUNT], first_of))
                v.tensor_copy(mark[:, 14:15], cact[:, 0:1]).then_inc(sem("meta"), 1)
                v.tensor_copy(mark[:, 2:3], cact[:, 0:1]).then_inc(sem("x_add"), 1)
                select(0)
                low_h(0)
                passes = dve.value_load(meta[0:1, COUNT:COUNT + 1], min_val=NE, max_val=2 * NE)
                with dve.Fori(0, passes) as p:
                    one_pass(p)
                add(passes, 0)
                add(passes, 1)
                dve.wait_ge(sem("x_add"), 2 * passes + 3)
                v.tensor_copy(mark[:, 15:16], cact[:, 0:1]).then_inc(sem("x_final"), 1)

            def low(p, j):
                dve.wait_ge(sem("w_hi"), p * HP + j + 1)
                v.tensor_tensor(wl[:, j % SPLITS, :], piece_half(j), wh[:, j % SPLITS, :].bitcast(F32),
                                ALU.subtract).then_inc(sem("w_lo"), 1)

            def low_h(p):
                for half in range(2):
                    dve.wait_ge(sem("hT_hi"), 2 * p + half + 1)
                    v.tensor_tensor(hTl[:, half * 4:half * 4 + 4, :].rearrange("p k n -> p (k n)"),
                                    ps[:, 2 + half, :],
                                    hTh[:, half * 4:half * 4 + 4, :].rearrange("p k n -> p (k n)").bitcast(F32),
                                    ALU.subtract).then_inc(sem("hT_lo"), 1)

            def select(p, weigh=(False, True)):
                e = dve.value_load(meta[0:1, bass.ds(p, 1)], min_val=0, max_val=NE - 1)
                second = dve.value_load(meta[0:1, bass.ds(p + TABLE, 1)], min_val=0, max_val=1)
                slots = iota[:, bass.ds(second * P, P)]
                for weighted in weigh:
                    if weighted:
                        dve.wait_ge(sem("gath_ps"), 2 * p + 2)
                    for t in range(NT):
                        place_ = posm[:, t, bass.ds(e, 1)]
                        last = v.tensor_scalar(sel[:, t, :], slots, place_, wts[:, t, bass.ds(e, 1)] if weighted
                                               else None, ALU.is_equal, *((ALU.mult,) if weighted else ()))
                    last.then_inc(sem("sel"), 1)

            def add(p, t):
                dve.wait_ge(sem("spread_ps"), 2 * p + t + 1)
                v.tensor_tensor(x[:, t, :], x[:, t, :], bank2(2), ALU.add).then_inc(sem("x_add"), 1)

            def one_pass(p):
                for j in range(HP):
                    if j in (0, 2):
                        add(p, j // 2)
                    if j == 10:
                        dve.wait_ge(sem("swT_ps"), p + 1)
                        select(p + 1, (False,))
                    if j in silu_after:
                        c = silu_after[j]
                        dve.wait_ge(sem("e_tanh"), p * ECHUNKS + c + 1)
                        b = 2 * (c % 2)
                        v.scalar_tensor_tensor(out=e_tg, in0=e_tg, scalar=1.0, in1=ps[:, b, :], op0=ALU.add,
                                               op1=ALU.mult).then_inc(sem("e_mid"), 1)
                        dve.wait_ge(sem("e_mid"), p * ECHUNKS + c + 1)
                        v.scalar_tensor_tensor(out=e_hid, in0=e_tg, scalar=0.5, in1=ps[:, b + 1, :], op0=ALU.mult,
                                               op1=ALU.mult).then_inc(sem("e_hid"), 1)
                    if j in turn_after:
                        c = turn_after[j]
                        dve.wait_ge(sem("fT_hi"), p * ECHUNKS + c + 1)
                        high, low_ = fT_parts(c)
                        v.tensor_tensor(low_, ps[:, 6 + c % 2, :], high.bitcast(F32), ALU.subtract)\
                            .then_inc(sem("fT_lo"), 1)
                    if j == GATHER_AFTER + 1:
                        select(p + 1, (True,))
                    if j == SPLIT_H_AFTER:
                        low_h(p + 1)
                    if j == HP - 1:
                        dve.wait_ge(sem("w_used"), (p + 1) * HP + SPLITS)
                        v.tensor_tensor(ynat, bank2(4), gate_row, ALU.mult).then_inc(sem("y_sb"), 1)
                    low(p, j + SPLITS)

            for l in range(DEPTH):
                mixer(l)
                if l == 0:
                    dense()
                else:
                    experts()


_INS = ["x", "c", "positions", "w_ada", "b_ada", "norm_gain", "w_in", "latent_gain", "w_q_up", "w_kv_up", "q_gain",
        "k_gain", "conv_w", "conv_b", "w_a", "b_a", "w_x", "b_x", "lru_lambda", "out_gain", "w_out", "ffn_w_gate",
        "ffn_w_up", "ffn_w_down", "router_w", "moe_w_gate", "moe_w_up", "moe_w_down"]


def kernel(**inputs):
    import concourse.bacc as bacc
    from concourse.bass_utils import run_bass_kernel_spmd

    nc = bacc.Bacc("TRN2", target_bir_lowering=False, num_devices=1)
    arrays, args = {}, []
    for name in _INS:
        a = np.ascontiguousarray(inputs[name])
        arrays[f"in_{name}"] = a
        args.append(nc.dram_tensor(f"in_{name}", a.shape, mybir.dt.from_np(a.dtype), kind="ExternalInput").ap())
    shape = arrays["in_x"].shape
    args.append(nc.dram_tensor("out_x", shape, F32, kind="ExternalOutput").ap())
    trunk(nc, *args)
    r = run_bass_kernel_spmd(nc, [arrays], core_ids=[0])
    return r.results[0]["out_x"]
```
